# Optimizing a Trainium2 kernel written in Bass

```python
import jax, jax.numpy as jnp
from jax import lax
import numpy as np

D_MODEL = 1024
BATCH = 1
SEQ = 128
DEPTH = 2
DEC_BATCH = 1
DEC_SEQ = 256
PAST_LEN = 128

GRID_W = 64
CHUNK = 128
QBLOCK = 128
WINDOW = 128
ROPE_THETA = 10000.0
EPS = 1e-6
NEG_INF = -1e30
A_WIDTH = 512
A_GROUPS = 4
A_GDIM = A_WIDTH // A_GROUPS
B_HEADS = 8
B_KV_HEADS = 2
B_GROUP = B_HEADS // B_KV_HEADS
B_HEAD_DIM = 64
B_WIDTH = B_HEADS * B_HEAD_DIM
B_SCALE = B_HEAD_DIM ** -0.5
EVEN_IN = 2 * A_WIDTH + B_WIDTH + 2 * B_KV_HEADS * B_HEAD_DIM
EVEN_SPLIT = (A_WIDTH, 2 * A_WIDTH, 2 * A_WIDTH + B_WIDTH, 2 * A_WIDTH + B_WIDTH + B_KV_HEADS * B_HEAD_DIM)
C_HEADS = 16
C_Q_LORA = 384
C_KV_LORA = 256
C_NOPE = 64
C_ROPE = 32
C_QK = C_NOPE + C_ROPE
C_V = 64
C_SCALE = C_QK ** -0.5
ODD_IN = C_Q_LORA + C_KV_LORA + C_ROPE
N_GROUPS = 4
EXPERTS_PER_GROUP = 8
N_EXPERTS = N_GROUPS * EXPERTS_PER_GROUP
TOP_K = 2
D_EXPERT = 256

kernel_name = "hybrid_diffusion_prefix_trunk_step"

f32 = jnp.float32

def rms_norm(x, g):
    xf = x.astype(f32)
    y = xf * lax.rsqrt(jnp.mean(xf * xf, -1, keepdims=True) + EPS)
    return (y * g.astype(f32)).astype(x.dtype)

def layer_norm(x, g):
    xf = x.astype(f32)
    mu = jnp.mean(xf, -1, keepdims=True)
    var = jnp.mean(jnp.square(xf - mu), -1, keepdims=True)
    return ((xf - mu) * lax.rsqrt(var + EPS) * g.astype(f32)).astype(x.dtype)

def adaln(cond, w, b):
    m = jax.nn.silu(cond) @ w + b
    return jnp.split(m[..., None, :], 6, axis=-1)

def axial_angles(n, rot_dim):
    rows_count = n // GRID_W
    rows = jnp.repeat(jnp.arange(rows_count), GRID_W).astype(f32)
    cols = jnp.tile(jnp.arange(GRID_W), rows_count).astype(f32)
    d_axis = rot_dim // 2
    inv = ROPE_THETA ** (-jnp.arange(0, d_axis, 2, dtype=f32) / d_axis)
    ang = jnp.concatenate([rows[:, None] * inv, cols[:, None] * inv], -1)
    return jnp.cos(ang), jnp.sin(ang)

def apply_rope(x, cos, sin):
    xf = x.astype(f32).reshape(x.shape[:-1] + (x.shape[-1] // 2, 2))
    x1, x2 = xf[..., 0], xf[..., 1]
    c, s = cos[:, None, :], sin[:, None, :]
    out = jnp.stack([x1 * c - x2 * s, x1 * s + x2 * c], -1).reshape(x.shape)
    return out.astype(x.dtype)

def softmax_sink(s, sink):
    if sink is None:
        return jax.nn.softmax(s, -1)
    sk = sink.astype(f32)[None, :, :, None, None]
    m = jnp.maximum(jnp.max(s, -1, keepdims=True), sk)
    e = jnp.exp(s - m)
    return e / (jnp.sum(e, -1, keepdims=True) + jnp.exp(sk - m))

def dense_attention(q, k, v, scale, sink):
    bn, nq, kvh, grp, _ = q.shape
    dv = v.shape[-1]
    nb = nq // QBLOCK
    kf, vf = k.astype(f32), v.astype(f32)
    qb = jnp.moveaxis(q.reshape(bn, nb, QBLOCK, kvh, grp, q.shape[-1]), 1, 0)

    def one(qi):
        s = jnp.einsum('bqkgd,bskd->bkgqs', qi.astype(f32), kf) * scale
        p = softmax_sink(s, sink)
        return jnp.einsum('bkgqs,bskd->bqkgd', p, vf).astype(v.dtype)

    o = lax.map(one, qb)
    return jnp.moveaxis(o, 0, 1).reshape(bn, nq, kvh * grp * dv)

def window_attention(q, k, v, kc, vc, scale, sink):
    bn, n, kvh, grp, dh = q.shape
    dv = v.shape[-1]
    nb = n // QBLOCK
    span = QBLOCK + 2 * WINDOW
    pad = ((0, 0), (WINDOW, WINDOW), (0, 0), (0, 0))
    kp = jnp.pad(k, pad).astype(f32)
    vp = jnp.pad(v, pad).astype(f32)
    kcf, vcf = kc.astype(f32), vc.astype(f32)
    qb = jnp.moveaxis(q.reshape(bn, nb, QBLOCK, kvh, grp, dh), 1, 0)

    def one(args):
        qi, start = args
        kw = lax.dynamic_slice_in_dim(kp, start, span, axis=1)
        vw = lax.dynamic_slice_in_dim(vp, start, span, axis=1)
        qpos = start + jnp.arange(QBLOCK)
        kpos = start - WINDOW + jnp.arange(span)
        valid = (jnp.abs(qpos[:, None] - kpos[None, :]) <= WINDOW) & (kpos >= 0) & (kpos < n)
        qf = qi.astype(f32)
        s_loc = jnp.where(valid, jnp.einsum('bqkgd,bskd->bkgqs', qf, kw) * scale, NEG_INF)
        s_ctx = jnp.einsum('bqkgd,bskd->bkgqs', qf, kcf) * scale
        p = softmax_sink(jnp.concatenate([s_loc, s_ctx], -1), sink)
        o = (jnp.einsum('bkgqs,bskd->bqkgd', p[..., :span], vw)
             + jnp.einsum('bkgqs,bskd->bqkgd', p[..., span:], vcf))
        return o.astype(v.dtype)

    o = lax.map(one, (qb, jnp.arange(nb) * QBLOCK))
    return jnp.moveaxis(o, 0, 1).reshape(bn, n, kvh * grp * dv)

def chunk_gmlp(u, v, g_vnorm, w_s, b_s):
    bn, n, _ = u.shape
    u = jax.nn.gelu(u)
    v = layer_norm(jax.nn.gelu(v), g_vnorm)
    vc = v.reshape(bn, n // CHUNK, CHUNK, A_GROUPS, A_GDIM)
    mixed = jnp.einsum('gts,bnsgc->bntgc', w_s, vc) + b_s.T[None, None, :, :, None]
    return u * mixed.reshape(bn, n, A_WIDTH)

def even_mixer(h, p, rope, ctx):
    bn, n, _ = h.shape
    z = h @ p['w_in']
    u, v, q, k, vv = jnp.split(z, EVEN_SPLIT, axis=-1)
    a_out = chunk_gmlp(u, v, p['g_vnorm'], p['w_s'], p['b_s'])
    q = rms_norm(q.reshape(bn, n, B_HEADS, B_HEAD_DIM), p['g_q'])
    k = rms_norm(k.reshape(bn, n, B_KV_HEADS, B_HEAD_DIM), p['g_k'])
    vv = vv.reshape(bn, n, B_KV_HEADS, B_HEAD_DIM)
    sink = p['sink'].reshape(B_KV_HEADS, B_GROUP)
    if ctx is None:
        b_out = dense_attention(q.reshape(bn, n, B_KV_HEADS, B_GROUP, B_HEAD_DIM), k, vv, B_SCALE, sink)
        state = (k, vv)
    else:
        cos, sin = rope
        q = apply_rope(q, cos, sin)
        k = apply_rope(k, cos, sin)
        b_out = window_attention(q.reshape(bn, n, B_KV_HEADS, B_GROUP, B_HEAD_DIM), k, vv,
                                 ctx[0], ctx[1], B_SCALE, sink)
        state = None
    return jnp.concatenate([a_out, b_out], -1) @ p['w_o'], state

def mla_expand(ckv, kpe, w_ukv, g_k):
    bn, n, _ = ckv.shape
    kv = (ckv @ w_ukv).reshape(bn, n, C_HEADS, C_NOPE + C_V)
    k_nope, v = kv[..., :C_NOPE], kv[..., C_NOPE:]
    k = jnp.concatenate([k_nope, jnp.broadcast_to(kpe[:, :, None, :], (bn, n, C_HEADS, C_ROPE))], -1)
    return rms_norm(k, g_k), v

def rope_tail(x, cos, sin):
    return jnp.concatenate([x[..., :C_NOPE], apply_rope(x[..., C_NOPE:], cos, sin)], -1)

def odd_mixer(h, p, rope, ctx):
    bn, n, _ = h.shape
    z = h @ p['w_in']
    cq, ckv, kpe = jnp.split(z, (C_Q_LORA, C_Q_LORA + C_KV_LORA), axis=-1)
    q = (rms_norm(cq, p['g_qa']) @ p['w_uq']).reshape(bn, n, C_HEADS, C_QK)
    q = rms_norm(q, p['g_q'])
    ckv = rms_norm(ckv, p['g_kva'])
    k, v = mla_expand(ckv, kpe, p['w_ukv'], p['g_k'])
    if ctx is None:
        out = dense_attention(q[:, :, :, None, :], k, v, C_SCALE, None)
        state = (ckv, kpe)
    else:
        cos, sin = rope
        q = rope_tail(q, cos, sin)
        k = rope_tail(k, cos, sin)
        kc, vc = mla_expand(ctx[0], ctx[1], p['w_ukv'], p['g_k'])
        out = dense_attention(q[:, :, :, None, :], jnp.concatenate([kc, k], 1),
                              jnp.concatenate([vc, v], 1), C_SCALE, None)
        state = None
    return out @ p['w_o'], state

def hier_moe(h, p):
    bn, n, d = h.shape
    t = h.reshape(-1, d)
    lg = (t @ p['w_rg']).astype(f32) + p['b_rg'].astype(f32)
    pg = jax.nn.softmax(lg, -1)
    _, gsel = lax.top_k(lg, 1)
    gmask = jax.nn.one_hot(gsel[:, 0], N_GROUPS, dtype=f32)
    pg_sel = jnp.sum(pg * gmask, -1)
    le = ((t @ p['w_re']).astype(f32) + p['b_re'].astype(f32)).reshape(-1, N_GROUPS, EXPERTS_PER_GROUP)
    pe = jax.nn.softmax(jnp.einsum('tg,tge->te', gmask, le), -1)
    wk, ik = lax.top_k(pe, TOP_K)
    wk = wk / jnp.sum(wk, -1, keepdims=True)
    w_grp = jnp.sum(jax.nn.one_hot(ik, EXPERTS_PER_GROUP, dtype=f32) * wk[..., None], 1)
    gate = (gmask[:, :, None] * pg_sel[:, None, None] * w_grp[:, None, :]).reshape(-1, N_EXPERTS)
    h1 = jnp.einsum('td,edf->tef', t, p['w1'])
    h3 = jnp.einsum('td,edf->tef', t, p['w3'])
    hh = jax.nn.silu(h1) * h3 * gate[:, :, None].astype(t.dtype)
    return jnp.einsum('tef,efd->td', hh, p['w2']).reshape(bn, n, d)

def trunk_layer(x, cond, p, mixer, rope, ctx):
    sh1, sc1, g1, sh2, sc2, g2 = adaln(cond, p['w_ada'], p['b_ada'])
    h = rms_norm(x, p['g_norm1']) * (1 + sc1) + sh1
    y, state = mixer(h, p, rope, ctx)
    x = x + g1 * y
    h = rms_norm(x, p['g_norm2']) * (1 + sc2) + sh2
    x = x + g2 * hier_moe(h, p)
    return x, state

def setup_inputs(seed: int = 0) -> dict:
    key = jax.random.key(seed)
    ks = iter(jax.random.split(key, 64))

    def nrm(shape, s):
        return jax.random.normal(next(ks), shape, f32) * s

    def gain(n):
        return 1.0 + nrm((n,), 0.1)

    D = D_MODEL
    inp = {}
    inp['x_prompt'] = nrm((BATCH, SEQ, D), 1.0)
    inp['x_sample'] = nrm((DEC_BATCH, DEC_SEQ, D), 1.0)
    inp['cache_l0_k'] = nrm((DEC_BATCH, PAST_LEN, B_KV_HEADS, B_HEAD_DIM), 1.0)
    inp['cache_l0_v'] = nrm((DEC_BATCH, PAST_LEN, B_KV_HEADS, B_HEAD_DIM), 1.0)
    inp['cache_l1_ckv'] = nrm((DEC_BATCH, PAST_LEN, C_KV_LORA), 1.0)
    inp['cache_l1_kpe'] = nrm((DEC_BATCH, PAST_LEN, C_ROPE), 1.0)
    inp['c'] = nrm((DEC_BATCH, D), 1.0)
    inp['c_ctx'] = nrm((D,), 1.0)
    inp['l0_g_norm1'] = gain(D)
    inp['l0_g_norm2'] = gain(D)
    inp['l0_w_ada'] = nrm((D, 6 * D), 0.5 * D ** -0.5)
    inp['l0_b_ada'] = nrm((6 * D,), 0.05)
    inp['l0_w_in'] = nrm((D, EVEN_IN), D ** -0.5)
    inp['l0_g_vnorm'] = gain(A_WIDTH)
    inp['l0_w_s'] = nrm((A_GROUPS, CHUNK, CHUNK), CHUNK ** -0.5)
    inp['l0_b_s'] = 1.0 + nrm((A_GROUPS, CHUNK), 0.1)
    inp['l0_g_q'] = gain(B_HEAD_DIM)
    inp['l0_g_k'] = gain(B_HEAD_DIM)
    inp['l0_sink'] = nrm((B_HEADS,), 0.5)
    inp['l0_w_o'] = nrm((A_WIDTH + B_WIDTH, D), (A_WIDTH + B_WIDTH) ** -0.5)
    inp['l0_w_rg'] = nrm((D, N_GROUPS), D ** -0.5)
    inp['l0_b_rg'] = nrm((N_GROUPS,), 0.01)
    inp['l0_w_re'] = nrm((D, N_EXPERTS), D ** -0.5)
    inp['l0_b_re'] = nrm((N_EXPERTS,), 0.01)
    inp['l0_w1'] = nrm((N_EXPERTS, D, D_EXPERT), D ** -0.5)
    inp['l0_w3'] = nrm((N_EXPERTS, D, D_EXPERT), D ** -0.5)
    inp['l0_w2'] = nrm((N_EXPERTS, D_EXPERT, D), D_EXPERT ** -0.5)
    inp['l1_g_norm1'] = gain(D)
    inp['l1_g_norm2'] = gain(D)
    inp['l1_w_ada'] = nrm((D, 6 * D), 0.5 * D ** -0.5)
    inp['l1_b_ada'] = nrm((6 * D,), 0.05)
    inp['l1_w_in'] = nrm((D, ODD_IN), D ** -0.5)
    inp['l1_g_qa'] = gain(C_Q_LORA)
    inp['l1_w_uq'] = nrm((C_Q_LORA, C_HEADS * C_QK), C_Q_LORA ** -0.5)
    inp['l1_g_kva'] = gain(C_KV_LORA)
    inp['l1_w_ukv'] = nrm((C_KV_LORA, C_HEADS * (C_NOPE + C_V)), C_KV_LORA ** -0.5)
    inp['l1_g_q'] = gain(C_QK)
    inp['l1_g_k'] = gain(C_QK)
    inp['l1_w_o'] = nrm((C_HEADS * C_V, D), (C_HEADS * C_V) ** -0.5)
    inp['l1_w_rg'] = nrm((D, N_GROUPS), D ** -0.5)
    inp['l1_b_rg'] = nrm((N_GROUPS,), 0.01)
    inp['l1_w_re'] = nrm((D, N_EXPERTS), D ** -0.5)
    inp['l1_b_re'] = nrm((N_EXPERTS,), 0.01)
    inp['l1_w1'] = nrm((N_EXPERTS, D, D_EXPERT), D ** -0.5)
    inp['l1_w3'] = nrm((N_EXPERTS, D, D_EXPERT), D ** -0.5)
    inp['l1_w2'] = nrm((N_EXPERTS, D_EXPERT, D), D_EXPERT ** -0.5)
    return inp

def reference(x_prompt, x_sample, cache_l0_k, cache_l0_v, cache_l1_ckv, cache_l1_kpe, c, c_ctx,
              l0_g_norm1, l0_g_norm2, l0_w_ada, l0_b_ada, l0_w_in, l0_g_vnorm, l0_w_s, l0_b_s,
              l0_g_q, l0_g_k, l0_sink, l0_w_o, l0_w_rg, l0_b_rg, l0_w_re, l0_b_re, l0_w1, l0_w3, l0_w2,
              l1_g_norm1, l1_g_norm2, l1_w_ada, l1_b_ada, l1_w_in, l1_g_qa, l1_w_uq, l1_g_kva, l1_w_ukv,
              l1_g_q, l1_g_k, l1_w_o, l1_w_rg, l1_b_rg, l1_w_re, l1_b_re, l1_w1, l1_w3, l1_w2):
    p0 = dict(g_norm1=l0_g_norm1, g_norm2=l0_g_norm2, w_ada=l0_w_ada, b_ada=l0_b_ada, w_in=l0_w_in,
              g_vnorm=l0_g_vnorm, w_s=l0_w_s, b_s=l0_b_s, g_q=l0_g_q, g_k=l0_g_k, sink=l0_sink,
              w_o=l0_w_o, w_rg=l0_w_rg, b_rg=l0_b_rg, w_re=l0_w_re, b_re=l0_b_re,
              w1=l0_w1, w3=l0_w3, w2=l0_w2)
    p1 = dict(g_norm1=l1_g_norm1, g_norm2=l1_g_norm2, w_ada=l1_w_ada, b_ada=l1_b_ada, w_in=l1_w_in,
              g_qa=l1_g_qa, w_uq=l1_w_uq, g_kva=l1_g_kva, w_ukv=l1_w_ukv, g_q=l1_g_q, g_k=l1_g_k,
              w_o=l1_w_o, w_rg=l1_w_rg, b_rg=l1_b_rg, w_re=l1_w_re, b_re=l1_b_re,
              w1=l1_w1, w3=l1_w3, w2=l1_w2)
    params = [p0, p1]
    mixers = [even_mixer, odd_mixer]
    caches = [(cache_l0_k, cache_l0_v), (cache_l1_ckv, cache_l1_kpe)]
    n_lat = x_sample.shape[1]
    ropes = [axial_angles(n_lat, B_HEAD_DIM), axial_angles(n_lat, C_ROPE)]

    y_prompt = x_prompt
    states = []
    for l in range(DEPTH):
        y_prompt, st = trunk_layer(y_prompt, c_ctx, params[l], mixers[l % 2], None, None)
        states.append(st)

    y_sample = x_sample
    for l in range(DEPTH):
        y_sample, _ = trunk_layer(y_sample, c, params[l], mixers[l % 2], ropes[l % 2], caches[l])

    new_l0_k, new_l0_v = states[0]
    new_l1_ckv, new_l1_kpe = states[1]
    return (y_prompt, y_sample, new_l0_k, new_l0_v, new_l1_ckv, new_l1_kpe)


_drawn_inputs = setup_inputs


def setup_inputs(seed=0):
    import zlib

    import numpy as np

    out = dict(_drawn_inputs(seed))
    spreads = {}
    factors = {'cache_l0_k': 4.11,
     'cache_l0_v': 3.186,
     'cache_l1_ckv': 3.452,
     'cache_l1_kpe': 6.626,
     'l0_g_vnorm': 2.789,
     'l0_b_s': 2.99,
     'l0_g_q': 7.854,
     'l0_sink': 64.0,
     'l0_b_rg': 8.0,
     'l0_b_re': 8.0,
     'l1_g_qa': 7.929,
     'l1_g_q': 8.0,
     'l1_g_k': 8.0,
     'l1_b_rg': 49.655,
     'l1_b_re': 32.03}
    for name, (base, spread) in spreads.items():
        noise = np.random.default_rng([zlib.crc32(name.encode()), seed]).standard_normal(out[name].shape)
        drawn = base * np.exp(spread * noise) if base else spread * noise
        out[name] = __import__('jax').numpy.asarray(drawn.astype(out[name].dtype))
    for name, factor in factors.items():
        out[name] = (out[name] * factor).astype(out[name].dtype)
    return out
```

```python
import math
from contextlib import ExitStack

import numpy as np
import concourse.bass as bass
from concourse import mybir

P = 128
D = 1024
KD = D // P
NT = 3
N_LAYERS = 2
EPS = 1e-6
NEG = -1e30
A_WIDTH = 512
A_GROUPS = 4
HD = 64
B_HEADS = 8
QKW = (B_HEADS + 2) * HD
EVEN_IN = 2 * A_WIDTH + QKW + 2 * HD
C_HEADS = 16
HALF = C_HEADS // 2
QK = 96
NOPE = 64
ROPE = 32
Q_LORA = 384
KV_LORA = 256
ODD_IN = Q_LORA + KV_LORA + ROPE
NG = 4
EPG = 8
NE = NG * EPG
DE = 256
SLOTS = 64
MAX_BLOCKS = NT * P // SLOTS
OVER = (2 * NT * P) // (SLOTS + 1)
NB = NE + 1 + OVER
RING = 12
SLOT = 2048

U_ADA = (0, 32)
U_WIN0 = 24
U_WO = (56, 164)
U_MOE = (60, 168)
U_WIN1 = 156
U_UQ = 159
U_UKV = 162
UNITS = 264

C_ID, C_TRI, C_SEL, C_MASK, C_R0, C_R1, C_IOTA, C_PRI8, C_PRI4, C_31 = (
    0, 128, 256, 512, 768, 1024, 1152, 1216, 1224, 1228)
C_N = 1260


def shape_constants():
    c = np.zeros((P, C_N), np.float32)
    i = np.arange(P)
    c[:, C_ID:C_ID + P] = np.eye(P)
    c[:, C_TRI:C_TRI + P] = i[:, None] < i[None, :]
    for cond in range(2):
        c[:, C_SEL + cond * P:C_SEL + (cond + 1) * P] = (i % 32 == cond)[:, None]
    c[:, C_MASK:C_MASK + P] = np.where(i[None, :] <= i[:, None], 0.0, NEG)
    c[:, C_MASK + P:C_MASK + 2 * P] = np.where(i[:, None] <= i[None, :], 0.0, NEG)
    for col, rot in ((C_R0, HD), (C_R1, ROPE)):
        half = rot // 2
        inv = np.float32(10000.0) ** (-np.arange(0, half, 2, dtype=np.float32) / np.float32(half))
        n = np.arange(2 * P)
        ang = np.concatenate([(n // 64).astype(np.float32)[:, None] * inv,
                              (n % 64).astype(np.float32)[:, None] * inv], -1).astype(np.float32)
        cos, sin = np.cos(ang), np.sin(ang)
        for t in range(2):
            at = col + t * 2 * rot
            c[:, at:at + rot] = np.repeat(cos[t * P:(t + 1) * P], 2, axis=1)
            c[:, at + rot:at + 2 * rot:2] = -sin[t * P:(t + 1) * P]
            c[:, at + rot + 1:at + 2 * rot:2] = sin[t * P:(t + 1) * P]
    c[:, C_IOTA:C_IOTA + 64] = np.arange(64)
    c[:, C_PRI8:C_PRI8 + EPG] = EPG - np.arange(EPG)
    c[:, C_PRI4:C_PRI4 + NG] = NG - np.arange(NG)
    c[:, C_31:C_31 + NE] = NE - 1 - np.arange(NE)
    return c


SEMS = """early_in late_in ov_turns_sp ov_turns_act filled fill_done v_out cache_in ring_full0 ring_full1 ring_full2 ring_full3 ring_full4 ring_full5
 ring_full6 ring_full7 ring_full8 ring_full9 ring_full10 ring_full11 units_used cond_ready
 tiles_cleared ws_in_psum ws_ready m_ready bc_in_psum bc_ready rms_ready h_ready hT_in_psum hT_act
 hT_dve z_in_psum z_act_done sums_ready roots_ready v_ready qk_ready k_out mixed_in_psum a_ready
 qkT_in_psum qkT_ready kc_in_psum scores_in_psum max_ready probs_ready pT_in_psum pT_act pT_dve
 att_in_psum att_ready catT_in_psum catT_act catT_dve y_in_psum x_updated
 z1_in_psum z1_sums z1_roots cqkv_ready cqkvT_in_psum cqkvT_ready l1_out prep_in_psum prep_squares
 prep_sums prep_roots prep_ready prepT_in_psum prepT_act prepT_dve
 logits_in_psum logits_ready gexp_in gexp_out eexp_in eexp_out picks_ready rank_in_psum nover_ready
 ofs_in_psum route_ready rows_ready gathered xT_ready silu_ready hh_ready hhT_in_psum
 hhT_ready y_evac y_out0 y_out1 moe_done_gather pair_rows0 pair_rows1 pair_rows2 pair_rows3 pair_rows4
 pair_rows5 pair_read out_done act_chain dve_chain
 ov_w0 ov_w1 ov_rows0 ov_rows1 ov_gathered0 ov_gathered1 ov_xT0 ov_xT1 ov_h0 ov_h1 ov_silu0 ov_silu1
 ov_hh0 ov_hh1 ov_hhT0 ov_hhT1 ov_hhTs0 ov_hhTs1 ov_y0 ov_y1 ov_evac0 ov_evac1 ov_out0 ov_out1""".split()


def trunk(nc, A, O, Y):
    f32, i32 = mybir.dt.float32, mybir.dt.int32
    ALU, ACT, AX = mybir.AluOpType, mybir.ActivationFunctionType, mybir.AxisListType.X
    ctx = ExitStack()
    with ctx:
        S = {name: ctx.enter_context(nc.semaphore(name)) for name in SEMS}
        ring_full = [S[f"ring_full{i}"] for i in range(RING)]

        def sb(name, *shape, dt=f32):
            return ctx.enter_context(nc.sbuf_tensor(name, [P, *shape], dt))

        ring = sb("ring", RING, SLOT)
        x = sb("x_tiles", NT, D)
        AB = sb("scale_shift", 4 * D)
        G = sb("gate_rows", 2, D)
        m = sb("modulation", N_LAYERS, 3, 512)
        gn = sb("norm_gains", N_LAYERS, 512)
        con = sb("constants", C_N)
        ones = sb("ones", P)
        gvn = sb("gvn", A_WIDTH)
        gqk = sb("gqk", QKW)
        wsT = sb("wsT", A_GROUPS, P)
        bsT = sb("bsT", A_GROUPS)
        sink = sb("sink", B_HEADS)
        gqa = sb("gqa", Q_LORA)
        gkva = sb("gkva", KV_LORA)
        gq1 = sb("gq1", QK)
        gk1 = sb("gk1", QK)
        wr = sb("wr", N_LAYERS, KD, NG + NE)
        br = sb("br", N_LAYERS, NG + NE)
        cT = sb("cT", 2, KD)
        scT = sb("scT", KD, 32)
        eps = sb("eps", 1)
        ss = sb("sums_of_squares", 64)
        st = sb("softmax_stats", 4, 16)
        W = sb("scratch", 10 * D)
        tabi = sb("pair_index", N_LAYERS, 6, dt=i32)
        ovi = sb("overflow_blocks", N_LAYERS, 16, dt=i32)
        gates = sb("gates", NT, 2)
        ps = ctx.enter_context(nc.psum_tensor("psum", [P, 8, 512], f32))

        ident = con[:, C_ID:C_ID + P]
        iota = con[:, C_IOTA:C_IOTA + 64]

        def view(tile, at, *shape):
            n = math.prod(shape)
            v = tile[:, at:at + n]
            if len(shape) == 1:
                return v
            names = "abc"[:len(shape)]
            return v.rearrange(f"p ({' '.join(names)}) -> p {' '.join(names)}",
                               **dict(zip(names[1:], shape[1:])))

        def over(ap, axis, shape):
            return ap.unsqueeze(axis).to_broadcast(shape)

        hT = view(W, 0, NT, KD, P)
        h3 = view(W, 3 * D, NT, D)
        cat0 = view(W, 3 * D, NT, D)
        ws = view(W, 6 * D, A_GROUPS, P)
        qT0 = view(W, 6 * D, NT, 4, P)
        kT0 = view(W, 7680, 4, P)
        v0 = view(W, 8192, 4, P)
        kc = view(W, 8704, P)
        ua = view(AB, 0, 2, A_WIDTH)
        va = view(AB, 1024, 2, A_WIDTH)
        qk = view(AB, 2048, QKW)
        sq0 = view(AB, 2688, QKW)
        rt0 = view(AB, 3328, QKW)
        probs0 = view(W, 0, 2, 2, 384)
        pT0 = view(W, 1536, 2, 3, 256)
        kT1 = view(W, 0, HALF, 3, P)
        v1 = view(W, 3072, 3, HALF, NOPE)
        qT1 = view(W, 4608, HALF, P)
        cqT = view(W, 5632, NT, 3, P)
        ckvT = view(W, 6784, 4, 2, P)
        kpe = view(W, 7808, 4, ROPE)
        ckvc = view(W, 7936, KV_LORA)
        cat1 = view(W, 8192, 2, D)
        cqn = view(AB, 0, NT, Q_LORA)
        ckvn = view(AB, NT * Q_LORA, NT, KV_LORA)
        kw = view(AB, 0, HALF, QK)
        sq1 = view(AB, 768, HALF, QK)
        rt1 = view(AB, 3072, HALF, ROPE)
        probs1 = view(AB, 0, 2, 2, 384)
        pT1 = view(AB, 1536, 2, 3, 256)
        tmp = view(AB, 1024, D)
        catT = view(AB, 2048, 2, KD, P)
        junk = view(W, 9216, D)
        hp = view(W, 0, NT, KD, P)
        hmod = view(W, 3072, D)
        h2T = view(W, 4096, 2, KD, P)
        xT = view(W, 3072, 2, KD, SLOTS)
        rows = view(W, 4096, 2, NT, SLOTS)
        silu = W[64:128, 4480:4736]
        hh = W[:, 4736:4992]
        hhT = view(W, 5120, 2, 2, SLOTS)
        ysb = view(W, 5376, 2, 512)
        pair = view(W, 0, 4, D)
        slotm = view(W, 6400, NT, NB)
        RB = 6400 + NT * NB

        def cond_of(t):
            return 0 if t == 0 else 1

        MIX0 = [(t, i) for t in range(NT) for i in range(4)]
        SWEEPS = [(s, hb, t) for s in range(2) for hb in range(2) for t in ((0,), (1, 2))[s]]

        def batches(l, sweep=None):
            if l == 0:
                return [(n, t, i) for n, (t, i) in enumerate(MIX0)]
            at = len(MIX0) + 4 * sweep
            return [(at + i, SWEEPS[sweep][2], i) for i in range(4)]

        PREPS = []
        for s in range(2):
            for hb in range(2):
                PREPS += [[("kv", s, hb, t, j) for j, t in enumerate(((0,), (3, 1, 2))[s])]
                          + [("q", s, hb, ((0,), (1, 2))[s][0], 0)]]
                if s == 1:
                    PREPS += [[("q", s, hb, 2, 0)]]
        PREP_AT = [sum(map(len, PREPS[:i])) for i in range(len(PREPS))]

        def bc_source(n):
            l, v, c, hf = n // 24, n % 24 // 4, n % 4 // 2, n % 2
            chunk = 2 * v + hf
            return l, chunk // 4, 32 * (chunk % 4), c, hf

        def bc_target(n):
            v, c, hf = n % 24 // 4, n % 4 // 2, n % 2
            if v % 3 == 2:
                return G[:, c, hf * 512:(hf + 1) * 512]
            at = ((1 - v % 3) * 2 + c) * D + hf * 512
            return AB[:, at:at + 512]

        block = ctx.enter_context(nc.Block())

        @block.sync
        def _(sp):
            def load(unit, dst_floats, src, dims=None):
                slot = unit % RING
                if unit >= RING:
                    sp.wait_ge(S["units_used"], unit - RING + 1)
                dst = ring[:, slot, 0:dst_floats]
                if dims:
                    dst = dst.rearrange("p (k n) -> p k n", k=dims)
                sp.dma_start(dst, src).then_inc(ring_full[slot], 16)

            def load_ada(l):
                for r in range(3):
                    for k in range(KD):
                        load(U_ADA[l] + r * KD + k, SLOT,
                             A[f"l{l}_w_ada"].rearrange("(p k) n -> k p n", k=KD)[k, :, r * SLOT:(r + 1) * SLOT])

            def load_wo(l):
                for k in range(4):
                    load(U_WO[l] + k, 2 * D,
                         A[f"l{l}_w_o"][2 * k * P:(2 * k + 2) * P, :].rearrange("(k p) n -> p k n", p=P), 2)

            def load_experts(l):
                w1, w3, w2 = (A[f"l{l}_{n}"] for n in ("w1", "w3", "w2"))
                with sp.Fori(0, NE // 4) as i:
                    for u in range(4):
                        e = i * 4 + u
                        for n, w in enumerate((w1, w3, w2)):
                            slot = 3 * u + n
                            sp.wait_ge(S["units_used"], i * RING + (U_MOE[l] + slot - RING + 1))
                            if n < 2:
                                src = w[bass.ds(e, 1)].rearrange("e (p k) f -> p (e k f)", k=KD)
                                dst = ring[:, slot, :]
                            else:
                                src = w[bass.ds(e, 1)].rearrange("e (k p) d -> p (e k) d", p=P)
                                dst = ring[:, slot, :].rearrange("p (k d) -> p k d", k=2)
                            sp.dma_start(dst, src).then_inc(ring_full[slot], 16)

            def overflow(l):
                sp.wait_ge(S["route_ready"], l + 1)
                count = sp.value_load(ovi[0:1, l, 15:16], min_val=0, max_val=OVER)
                sp.wait_ge(S["units_used"], U_MOE[l] + 87)
                with sp.Fori(0, OVER) as b:
                    with sp.If(b < count):
                        e = sp.value_load(ovi[0:1, l, bass.ds(b, 1)], min_val=0, max_val=NE - 1)
                        for n, name in enumerate(("w1", "w3", "w2")):
                            w = A[f"l{l}_{name}"]
                            if n < 2:
                                src = w[bass.ds(e, 1)].rearrange("e (p k) f -> p (e k f)", k=KD)
                                dst = ring[:, n, :]
                            else:
                                src = w[bass.ds(e, 1)].rearrange("e (k p) d -> p (e k) d", p=P)
                                dst = ring[:, n, :].rearrange("p (k d) -> p k d", k=2)
                            sp.dma_start(dst, src).then_inc(S[f"ov_w{l}"], 16)
                        sp.wait_ge(S[f"ov_evac{l}"], b + 1)
                        sp.sem_inc(S["ov_turns_sp"], 1)
                    sp.end_ifs()

            load_ada(0)
            for k in range(KD):
                load(U_WIN0 + k, EVEN_IN, A["l0_w_in"][k * P:(k + 1) * P, :])
            load_ada(1)
            load_wo(0)
            load_experts(0)
            overflow(0)
            for n, (k0, k1) in enumerate(((0, 3), (3, 6), (6, 8))):
                load(U_WIN1 + n, (k1 - k0) * ODD_IN,
                     A["l1_w_in"][k0 * P:k1 * P, :].rearrange("(k p) n -> p k n", p=P), k1 - k0)
            for k in range(3):
                load(U_UQ + k, C_HEADS * QK, A["l1_w_uq"][k * P:(k + 1) * P, :])
            for k in range(2):
                load(U_UKV + k, SLOT, A["l1_w_ukv"][k * P:(k + 1) * P, :])
            load_wo(1)
            load_experts(1)
            overflow(1)

        @block.tensor
        def _(pe):
            def arrived(unit):
                pe.wait_ge(ring_full[unit % RING], 16 * (unit // RING + 1))

            def ada_unit(l, n):
                r, k = divmod(n, KD)
                unit = U_ADA[l] + n
                arrived(unit)
                if n == 0 and l == 0:
                    pe.wait_ge(S["cond_ready"], 1)
                if k == 0 and 3 * l + r > 0:
                    pe.wait_ge(S["m_ready"], 3 * l + r)
                for j in range(4):
                    last = nc.tensor.matmul(ps[32 * j:32 * j + 32, 7, :], scT[:, k, :],
                                            ring[:, unit % RING, j * 512:(j + 1) * 512],
                                            start=k == 0, stop=k == KD - 1)
                last.then_inc(S["units_used"], 1)

            def broadcasts(first, count):
                for n in range(first, first + count):
                    l, r, row, c, hf = bc_source(n)
                    pe.wait_ge(S["m_ready"], 3 * l + r + 1)
                    if n >= 4:
                        pe.wait_ge(S["bc_ready"], n - 3)
                    nc.tensor.matmul(ps[:, n % 4, :], con[row:row + 32, C_SEL + c * P:C_SEL + (c + 1) * P],
                                     m[row:row + 32, l, r, :], start=True, stop=True)\
                        .then_inc(S["bc_in_psum"], 1)

            def transpose_h(stage, src, permuted=False):
                pe.wait_ge(S["bc_ready"], 12 * (stage + 1))
                for t in range(NT):
                    pe.wait_ge(S["h_ready"], 3 * stage + t + 1)
                    for k in range(KD):
                        chunk = src[:, t, k, :] if permuted else src[:, t, k * P:(k + 1) * P]
                        last = nc.tensor.transpose(ps[:, 2 * t + k // 4, k % 4 * P:(k % 4 + 1) * P], chunk, ident)
                    last.then_inc(S["hT_in_psum"], 1)

            def wait_hT(stage, tiles=NT):
                pe.wait_ge(S["hT_act"], 3 * stage + tiles)
                pe.wait_ge(S["hT_dve"], 3 * stage + tiles)

            def scores(l, b):
                gb, t, i = b
                if gb >= 2:
                    pe.wait_ge(S["probs_ready"], gb - 1)
                par = gb % 2
                nk = P if t == 0 else 384
                for hd in range(2):
                    out = ps[:, 2 * par + hd, 0:nk]
                    if l == 0:
                        half = slice(64 * hd, 64 * hd + 64)
                        key0 = 0 if t == 0 else 1
                        keys = kT0[half, key0:key0 + nk // P, :]
                        last = nc.tensor.matmul(out, qT0[half, t, i, :], keys, start=True, stop=True)
                    else:
                        head = 2 * i + hd
                        last = nc.tensor.matmul(out, qT1[0:QK, head, :], kT1[0:QK, head, 0:nk // P, :],
                                                start=True, stop=True)
                last.then_inc(S["scores_in_psum"], 1)

            def transpose_probs(l, b):
                gb, t, i = b
                par = gb % 2
                pe.wait_ge(S["probs_ready"], gb + 1)
                if gb >= 1:
                    pe.wait_ge(S["pT_act"], gb)
                    pe.wait_ge(S["pT_dve"], gb)
                probs = (probs0, probs1)[l]
                for kt in range(1 if t == 0 else 3):
                    for hd in range(2):
                        at = hd * 512 if t == 0 else (2 * kt + hd) * P
                        last = nc.tensor.transpose(ps[:, 4 + at // 512, at % 512:at % 512 + P],
                                                   probs[:, par, hd, kt * P:(kt + 1) * P], ident)
                last.then_inc(S["pT_in_psum"], 1)

            def weighted_values(l, b):
                gb, t, i = b
                par = gb % 2
                pe.wait_ge(S["pT_act"], gb + 1)
                pe.wait_ge(S["pT_dve"], gb + 1)
                if gb >= 1:
                    pe.wait_ge(S["att_ready"], gb)
                pT = (pT0, pT1)[l]
                tiles = 1 if t == 0 else 3
                for hd in range(2):
                    for kt in range(tiles):
                        if l == 0:
                            v = v0[:, kt + (0 if t == 0 else 1), hd * HD:(hd + 1) * HD]
                        else:
                            v = v1[:, kt, 2 * i + hd, :]
                        last = nc.tensor.matmul(ps[:, 6, hd * HD:(hd + 1) * HD],
                                                pT[:, par, kt, hd * P:(hd + 1) * P], v,
                                                start=kt == 0, stop=kt == tiles - 1)
                last.then_inc(S["att_in_psum"], 1)

            def attention(l, todo, between=None):
                scores(l, todo[0])
                for n, b in enumerate(todo):
                    if n + 1 < len(todo):
                        scores(l, todo[n + 1])
                    if between:
                        between(n)
                    transpose_probs(l, b)
                    if n:
                        weighted_values(l, todo[n - 1])
                weighted_values(l, todo[-1])

            def out_projection(l, n, t, src, release):
                base = 2 * (n % 2)
                pe.wait_ge(S["att_ready"], att_count(l, t))
                if n == 1:
                    pe.wait_ge(S["m_ready"], 6)
                for k in range(KD):
                    last = nc.tensor.transpose(ps[:, base + k // 4, k % 4 * P:(k % 4 + 1) * P],
                                               src[:, k * P:(k + 1) * P], ident)
                    if n == 4 and k == 0:
                        last.then_inc(S["units_used"], 5)
                last.then_inc(S["catT_in_psum"], 1)
                pe.wait_ge(S["catT_act"], n + 1)
                pe.wait_ge(S["catT_dve"], n + 1)
                for k in range(KD):
                    if t in (0, 1, 2) and k % 2 == 0:
                        arrived(U_WO[l] + k // 2)
                    for hf in range(2):
                        last = nc.tensor.matmul(ps[:, 4 + base + hf, :],
                                                catT[:, n % 2, k, :],
                                                ring[:, (U_WO[l] + k // 2) % RING,
                                                     k % 2 * D + hf * 512:k % 2 * D + (hf + 1) * 512],
                                                start=k == 0, stop=k == KD - 1)
                    if release and k % 2:
                        last.then_inc(S["units_used"], 1)
                if not release:
                    last.then_inc(S["y_in_psum"], 1)

            def gather(l, e, par):
                for k in range(KD):
                    for t in range(NT):
                        last = nc.tensor.matmul(ps[:, par, k * SLOTS:(k + 1) * SLOTS], hp[:, t, k, :],
                                                rows[:, par, t, :], start=t == 0, stop=t == NT - 1)
                return last

            def up(par, slot):
                for k in range(KD):
                    for n in range(2):
                        last = nc.tensor.matmul(ps[64 * n:64 * n + 64, 2 + par, 0:DE], xT[:, par, k, :],
                                                ring[:, slot + n, k * DE:(k + 1) * DE],
                                                start=k == 0, stop=k == KD - 1)
                return last

            def transpose_hh():
                for k in range(2):
                    last = nc.tensor.transpose(ps[:, 4, k * P:(k + 1) * P], hh[:, k * P:(k + 1) * P], ident)
                return last

            def down(par, slot):
                for k in range(2):
                    for n in range(2):
                        last = nc.tensor.matmul(ps[64 * n:64 * n + 64, 5 + par, :], hhT[:, par, k, :],
                                                ring[:, slot, k * D + n * 512:k * D + (n + 1) * 512],
                                                start=k == 0, stop=k == 1)
                return last

            def experts(l):
                pe.wait_ge(S["rows_ready"], l * (NE + 1) + 1)
                gather(l, 0, 0).then_inc(S["gathered"], 1)
                with pe.Fori(0, NE // 4) as i:
                    for u in range(4):
                        par = u % 2
                        e = i * 4 + u
                        turn = (U_MOE[l]) // RING
                        pe.wait_ge(S["xT_ready"], e + (l * NE + 1))
                        for n in range(2):
                            pe.wait_ge(ring_full[3 * u + n], i * 16 + 16 * (turn + 1))
                        up(par, 3 * u).then_inc(S["units_used"], 2)
                        pe.wait_ge(S["rows_ready"], e + (l * (NE + 1) + 2))
                        gather(l, e + 1, 1 - par).then_inc(S["gathered"], 1)
                        pe.wait_ge(S["hh_ready"], e + (l * NE + 1))
                        transpose_hh().then_inc(S["hhT_in_psum"], 1)
                        pe.wait_ge(S["hhT_ready"], e + (l * NE + 1))
                        pe.wait_ge(ring_full[3 * u + 2], i * 16 + 16 * (turn + 1))
                        pe.wait_ge(S["y_evac"], e + (l * NE + 1))
                        down(par, 3 * u + 2).then_inc(S["units_used"], 1)

            def overflow(l):
                pe.wait_ge(S["route_ready"], l + 1)
                count = pe.value_load(ovi[0:1, l, 15:16], min_val=0, max_val=OVER)
                with pe.Fori(0, OVER) as b:
                    with pe.If(b < count):
                        pe.wait_ge(S[f"ov_rows{l}"], b + 1)
                        gather(l, None, 0).then_inc(S[f"ov_gathered{l}"], 1)
                        pe.wait_ge(S[f"ov_xT{l}"], b + 1)
                        pe.wait_ge(S[f"ov_w{l}"], b * 48 + 48)
                        up(0, 0).then_inc(S[f"ov_h{l}"], 1)
                        pe.wait_ge(S[f"ov_hh{l}"], b + 1)
                        transpose_hh().then_inc(S[f"ov_hhT{l}"], 1)
                        pe.wait_ge(S[f"ov_hhTs{l}"], b + 1)
                        down(0, 2).then_inc(S[f"ov_y{l}"], 1)
                    pe.end_ifs()

            def router(l):
                for t in range(NT):
                    wait_hT(2 * l + 1, t + 1)
                    for k in range(KD):
                        last = nc.tensor.matmul(ps[:, 6, t * 36:(t + 1) * 36], h2T[:, t % 2, k, :],
                                                wr[:, l, k, :], start=k == 0, stop=k == KD - 1)
                    last.then_inc(S["logits_in_psum"], 1)
                pe.wait_ge(S["picks_ready"], l + 1)
                picks = view(W, RB, NT, NE)
                tri = con[:, C_TRI:C_TRI + P]
                for t in range(NT):
                    for s in range(t + 1):
                        nc.tensor.matmul(ps[:, 7, t * NE:(t + 1) * NE], tri if s == t else ones[:, :],
                                         picks[:, s, :], start=s == 0, stop=s == t)
                for s in range(NT):
                    last = nc.tensor.matmul(ps[:, 7, NT * NE:(NT + 1) * NE], ones[:, :], picks[:, s, :],
                                            start=s == 0, stop=s == NT - 1)
                last.then_inc(S["rank_in_psum"], 1)
                pe.wait_ge(S["nover_ready"], l + 1)
                nc.tensor.matmul(ps[:, 6, 0:NE], view(W, RB + 300, P)[0:NE, :], con[0:NE, C_TRI:C_TRI + NE],
                                 start=True, stop=True).then_inc(S["ofs_in_psum"], 1)

            def att_count(l, t):
                if l == 0:
                    return 4 * (t + 1)
                last = max(n for n, w in enumerate(SWEEPS) if w[2] == t)
                return len(MIX0) + 4 * (last + 1)

            pe.wait_ge(S["early_in"], EARLY * 16)
            pe.wait_ge(S["tiles_cleared"], 2)
            for n in range(KD):
                ada_unit(0, n)
            pe.wait_ge(S["late_in"], LATE * 16)
            for g in range(A_GROUPS):
                last = nc.tensor.transpose(ps[:, 5, g * P:(g + 1) * P], ws[:, g, :], ident)
            last.then_inc(S["ws_in_psum"], 1)
            nc.tensor.transpose(ps[:, 6, 0:P], kc[:, :], ident).then_inc(S["kc_in_psum"], 1)
            for n in range(KD, 3 * KD):
                ada_unit(0, n)
            broadcasts(0, 12)
            transpose_h(0, h3)

            def project0(t):
                wait_hT(0)
                base = 4 * (t > 0)
                if t == 2:
                    pe.wait_ge(S["z_act_done"], 2)
                    pe.wait_ge(S["qk_ready"], 2)
                for k in range(KD):
                    arrived(U_WIN0 + k)
                    for n in range(4):
                        w = min(512, EVEN_IN - n * 512)
                        last = nc.tensor.matmul(ps[:, base + n, 0:w], hT[:, t, k, :],
                                                ring[:, (U_WIN0 + k) % RING, n * 512:n * 512 + w],
                                                start=k == 0, stop=k == KD - 1)
                    if t == 2:
                        last.then_inc(S["units_used"], 1)
                if t < 2:
                    last.then_inc(S["z_in_psum"], 1)

            def after0(t):
                pe.wait_ge(S["v_ready"], t + 1)
                pe.wait_ge(S["ws_ready"], 1)
                if t:
                    pe.wait_ge(S["a_ready"], t)
                for g in range(A_GROUPS):
                    last = nc.tensor.matmul(ps[:, 0, g * P:(g + 1) * P], wsT[:, g, :],
                                            va[:, t % 2, g * P:(g + 1) * P], start=True, stop=True)
                last.then_inc(S["mixed_in_psum"], 1)
                pe.wait_ge(S["qk_ready"], t + 1)
                if t:
                    pe.wait_ge(S["qkT_ready"], t)
                for i in range(5):
                    out = ps[:, 1, i * P:(i + 1) * P] if i < 4 else ps[:, 2, 0:P]
                    last = nc.tensor.transpose(out, qk[:, i * P:(i + 1) * P], ident)
                last.then_inc(S["qkT_in_psum"], 1)

            project0(0)
            project0(1)
            after0(0)
            project0(2)
            after0(1)
            after0(2)
            pe.wait_ge(S["qkT_ready"], 3)
            pe.wait_ge(S["a_ready"], 3)
            attention(0, batches(0), lambda n: [ada_unit(1, 2 * n), ada_unit(1, 2 * n + 1)])
            for t in range(NT):
                out_projection(0, t, t, cat0[:, t, :], t == 2)
            broadcasts(12, 12)
            transpose_h(1, hp, True)
            router(0)
            experts(0)
            overflow(0)

            broadcasts(24, 12)
            transpose_h(2, h3)
            for t in range(NT):
                wait_hT(2)
                for k in range(KD):
                    u, c = divmod(k, 3)
                    arrived(U_WIN1 + u)
                    for n, (c0, c1) in enumerate(((0, Q_LORA), (Q_LORA, ODD_IN))):
                        last = nc.tensor.matmul(ps[:, 2 * t + n, 0:c1 - c0], hT[:, t, k, :],
                                                ring[:, (U_WIN1 + u) % RING, c * ODD_IN + c0:c * ODD_IN + c1],
                                                start=k == 0, stop=k == KD - 1)
                    if t == 2 and k in (2, 5, 7):
                        last.then_inc(S["units_used"], 1)
                if t < 2:
                    last.then_inc(S["z1_in_psum"], 1)
            pe.wait_ge(S["cache_in"], 32)
            for t in (3, 0, 1, 2):
                if t < 3:
                    pe.wait_ge(S["cqkv_ready"], t + 1)
                    for k in range(3):
                        nc.tensor.transpose(ps[:, 2 * t, k * P:(k + 1) * P], cqn[:, t, k * P:(k + 1) * P], ident)
                for k in range(2):
                    src = ckvc if t == 3 else ckvn[:, t, :]
                    last = nc.tensor.transpose(ps[:, 2 * t + (t < 3), k * P:(k + 1) * P],
                                               src[:, k * P:(k + 1) * P], ident)
                last.then_inc(S["cqkvT_in_psum"], 1)

            def expand(n, prep):
                kind, s, hb, t, j = prep
                base = 2 * (n % 2)
                if kind == "kv":
                    for k in range(2):
                        arrived(U_UKV + k)
                        for q in range(2):
                            at = hb * 1024 + q * 512
                            last = nc.tensor.matmul(ps[:, base + q, :], ckvT[:, t, k, :],
                                                    ring[:, (U_UKV + k) % RING, at:at + 512],
                                                    start=k == 0, stop=k == 1)
                else:
                    for k in range(3):
                        arrived(U_UQ + k)
                        for q in range(2):
                            at = hb * 768 + q * 384
                            last = nc.tensor.matmul(ps[:, base + q, 0:384], cqT[:, t, k, :],
                                                    ring[:, (U_UQ + k) % RING, at:at + 384],
                                                    start=k == 0, stop=k == 2)
                last.then_inc(S["prep_in_psum"], 1)

            def transpose_prep(n):
                pe.wait_ge(S["prep_ready"], n + 1)
                if n >= 2:
                    pe.wait_ge(S["prepT_act"], n - 1)
                    pe.wait_ge(S["prepT_dve"], n - 1)
                for h in range(HALF):
                    last = nc.tensor.transpose(ps[0:QK, 4 + 2 * (n % 2) + h // 4, h % 4 * P:(h % 4 + 1) * P],
                                               kw[:, h, :], ident)
                last.then_inc(S["prepT_in_psum"], 1)

            pe.wait_ge(S["cqkvT_ready"], 4)
            for sweep, preps in enumerate(PREPS):
                at = PREP_AT[sweep]
                expand(at, preps[0])
                for n, prep in enumerate(preps):
                    if n + 1 < len(preps):
                        expand(at + n + 1, preps[n + 1])
                    transpose_prep(at + n)
                pe.wait_ge(S["prepT_act"], at + len(preps))
                pe.wait_ge(S["prepT_dve"], at + len(preps))
                attention(1, batches(1, sweep))
                if sweep == 1:
                    out_projection(1, 3, 0, cat1[:, 0, :], False)
            for t in (1, 2):
                out_projection(1, 3 + t, t, cat1[:, t - 1, :], t == 2)
            broadcasts(36, 12)
            transpose_h(3, hp, True)
            router(1)
            experts(1)
            overflow(1)

        @block.scalar
        def _(act):
            chain = [0]

            def link(ins):
                chain[0] += 1
                ins.then_inc(S["act_chain"], 1)
                act.wait_ge(S["act_chain"], chain[0])

            def spread(vec, n):
                return vec.rearrange("(a n) -> a n", a=1).to_broadcast([P, n])

            def early(dst, src):
                act.dma_start(dst, src).then_inc(S["early_in"], 16)

            def late(dst, src):
                act.dma_start(dst, src).then_inc(S["late_in"], 16)

            early(cT[:, 0, :], A["c_ctx"].rearrange("(p k) -> p k", p=P))
            early(cT[:, 1, :], A["c"].rearrange("a (p k) -> p (a k)", p=P))
            early(con[:, :], A["shape_constants"])
            act.wait_ge(S["tiles_cleared"], 1)
            for l in range(N_LAYERS):
                bias = A[f"l{l}_b_ada"].rearrange("(r j n) -> j r n", r=3, j=4)
                for j in range(4):
                    early(m[32 * j:32 * j + 2, l], bias[j:j + 1].to_broadcast([2, 3, 512]))
                for row, name, hf in ((0, "g_norm2", 0), (32, "g_norm2", 1), (64, "g_norm1", 0), (96, "g_norm1", 1)):
                    early(gn[row:row + 2, l], A[f"l{l}_{name}"][hf * 512:(hf + 1) * 512]
                          .rearrange("(a n) -> a n", a=1).to_broadcast([2, 512]))
            late(x[:, 0, :], A["x_prompt"].rearrange("a s d -> (a s) d"))
            late(x[:, 1:3, :], A["x_sample"].rearrange("a (t s) d -> s (a t) d", t=2))
            late(ws[:, :, :], A["l0_w_s"].rearrange("g t s -> t g s"))
            late(kc[:, :], A["cache_l0_k"].rearrange("a s h d -> (a s) (h d)"))
            late(v0[:, 1, :], A["cache_l0_v"].rearrange("a s h d -> (a s) (h d)"))
            late(gvn[:, :], spread(A["l0_g_vnorm"], A_WIDTH))
            for n in range(B_HEADS + 2):
                late(gqk[:, n * HD:(n + 1) * HD], spread(A["l0_g_q" if n < B_HEADS else "l0_g_k"], HD))
            with nc.allow_non_contiguous_dma(reason="512 words"):
                late(bsT[:, :], A["l0_b_s"].rearrange("g t -> t g"))
            late(sink[:, :], spread(A["l0_sink"], B_HEADS))
            late(gqa[:, :], spread(A["l1_g_qa"], Q_LORA))
            late(gkva[:, :], spread(A["l1_g_kva"], KV_LORA))
            late(gq1[:, :], spread(A["l1_g_q"], QK))
            late(gk1[:, :], spread(A["l1_g_k"], QK))
            for l in range(N_LAYERS):
                late(wr[:, l, :, 0:NG], A[f"l{l}_w_rg"].rearrange("(p k) n -> p k n", k=KD))
                late(wr[:, l, :, NG:], A[f"l{l}_w_re"].rearrange("(p k) n -> p k n", k=KD))
                late(br[:, l, 0:NG], spread(A[f"l{l}_b_rg"], NG))
                late(br[:, l, NG:], spread(A[f"l{l}_b_re"], NE))

            act.wait_ge(S["early_in"], EARLY * 16)
            act.wait_ge(S["tiles_cleared"], 2)
            nc.scalar.activation(scT[:, :, 0:2], cT[:, :, :].rearrange("p c k -> p k c"), ACT.Silu)\
                .then_inc(S["cond_ready"], 1)
            act.wait_ge(S["ws_in_psum"], 1)
            nc.scalar.copy(wsT[:, :, :], ps[:, 5, :].rearrange("p (g t) -> p g t", g=A_GROUPS))\
                .then_inc(S["ws_ready"], 1)
            act.wait_ge(S["kc_in_psum"], 1)
            link(nc.scalar.copy(kT0[:, 1, :], ps[:, 6, 0:P]))

            def rms(stage):
                if stage:
                    act.wait_ge(S["x_updated"], 3 * stage)
                for t in range(NT):
                    link(nc.scalar.activation(junk[:, :], x[:, t, :], ACT.Square, accum_out=ss[:, t:t + 1]))
                nc.scalar.activation(ss[:, 4:7], ss[:, 0:3], ACT.Sqrt, bias=eps[:, :], scale=1.0 / D)\
                    .then_inc(S["rms_ready"], 1)

            def broadcasts(first, count):
                for n in range(first, first + count):
                    if n == 12 or n == 24 or n == 36:
                        act.wait_ge(S["x_updated"], n // 4)
                    act.wait_ge(S["bc_in_psum"], n + 1)
                    nc.scalar.copy(bc_target(n), ps[:, n % 4, :]).then_inc(S["bc_ready"], 1)

            def evac_h(stage, dst, dbuf):
                for t in range(NT):
                    act.wait_ge(S["hT_in_psum"], 3 * stage + t + 1)
                    if dbuf and t == 2:
                        act.wait_ge(S["logits_in_psum"], 3 * (stage // 2) + 1)
                    nc.scalar.copy(dst[:, t % 2 if dbuf else t, 0:4, :],
                                   ps[:, 2 * t, :].rearrange("p (k q) -> p k q", k=4)).then_inc(S["hT_act"], 1)

            def exps(l, b):
                gb, t, i = b
                par = gb % 2
                probs = (probs0, probs1)[l]
                nk = P if t == 0 else 384
                act.wait_ge(S["max_ready"], gb + 1)
                if gb >= 2:
                    act.wait_ge(S["pT_in_psum"], gb - 1)
                if l == 0:
                    nc.scalar.activation(st[:, gb % 4, 8:10], st[:, gb % 4, 6:8], ACT.Exp)
                scale = HD ** -0.5 if l == 0 else QK ** -0.5
                for hd in range(2):
                    last = nc.scalar.activation(probs[:, par, hd, 0:nk], ps[:, 2 * par + hd, 0:nk], ACT.Exp,
                                                bias=st[:, gb % 4, 4 + hd:5 + hd], scale=scale,
                                                accum_out=st[:, gb % 4, 10 + hd:11 + hd])
                last.then_inc(S["probs_ready"], 1)

            def evac_pT(l, b):
                gb, t, i = b
                par = gb % 2
                pT = (pT0, pT1)[l]
                act.wait_ge(S["pT_in_psum"], gb + 1)
                if gb >= 2:
                    act.wait_ge(S["att_in_psum"], gb - 1)
                if t == 0:
                    nc.scalar.copy(pT[:, par, 0, 0:P], ps[:, 4, 0:P]).then_inc(S["pT_act"], 1)
                else:
                    nc.scalar.copy(pT[:, par, 0:2, :], ps[:, 4, :].rearrange("p (k n) -> p k n", k=2))\
                        .then_inc(S["pT_act"], 1)

            def attention(l, todo):
                exps(l, todo[0])
                for n, b in enumerate(todo):
                    if n + 1 < len(todo):
                        exps(l, todo[n + 1])
                    evac_pT(l, b)

            def evac_cat(n):
                act.wait_ge(S["catT_in_psum"], n + 1)
                if n >= 2:
                    act.wait_ge(S["x_updated"], x_after(n - 2))
                nc.scalar.copy(catT[:, n % 2, 0:4, :],
                               ps[:, 2 * (n % 2), :].rearrange("p (k q) -> p k q", k=4)).then_inc(S["catT_act"], 1)

            def experts(l):
                turns = l * NE // 2
                with act.Fori(0, NE // 4) as i:
                    for u in range(4):
                        par = u % 2
                        e = i * 4 + u
                        act.wait_ge(S["units_used"], i * RING + (U_MOE[l] + 3 * u + 2))
                        nc.scalar.activation(silu, ps[0:64, 2 + par, 0:DE], ACT.Silu).then_inc(S["silu_ready"], 1)
                        act.wait_ge(S["hhT_in_psum"], e + (l * NE + 1))
                        nc.scalar.copy(hhT[:, par, :, :], ps[:, 4, 0:2 * P].rearrange("p (k s) -> p k s", k=2)[:, :, SLOTS:])\
                            .then_inc(S["hhT_ready"], 1)
                        act.wait_ge(S["units_used"], i * RING + (U_MOE[l] + 3 * u + 3))
                        act.wait_ge(S[f"y_out{par}"], i * 64 + 32 * (turns + u // 2 + 1))
                        nc.scalar.copy(ysb[:, par, :], ps[:, 5 + par, :]).then_inc(S["y_evac"], 1)
                        act.wait_ge(S["y_evac"], e + (l * NE + 3))
                        for n in range(2):
                            act.dma_start(Y[bass.ds(e * SLOTS, SLOTS), n * 512:(n + 1) * 512],
                                          ysb[64 * n:64 * n + 64, par, :]).then_inc(S[f"y_out{par}"], 16)

            def overflow(l):
                act.wait_ge(S["route_ready"], l + 1)
                count = act.value_load(ovi[0:1, l, 15:16], min_val=0, max_val=OVER)
                act.wait_ge(S["y_out0"], 32 * ((l + 1) * NE // 2 + 1))
                act.wait_ge(S["y_out1"], 32 * ((l + 1) * NE // 2 + 1))
                with act.Fori(0, OVER) as b:
                    with act.If(b < count):
                        act.wait_ge(S[f"ov_h{l}"], b + 1)
                        nc.scalar.activation(silu, ps[0:64, 2, 0:DE], ACT.Silu).then_inc(S[f"ov_silu{l}"], 1)
                        act.wait_ge(S[f"ov_hhT{l}"], b + 1)
                        nc.scalar.copy(hhT[:, 0, :, :], ps[:, 4, 0:2 * P].rearrange("p (k s) -> p k s", k=2)[:, :, SLOTS:])\
                            .then_inc(S[f"ov_hhTs{l}"], 1)
                        act.wait_ge(S[f"ov_y{l}"], b + 1)
                        nc.scalar.copy(ysb[:, 0, :], ps[:, 5, :]).then_inc(S[f"ov_evac{l}"], 1)
                        act.wait_ge(S[f"ov_evac{l}"], b + 1)
                        for n in range(2):
                            act.dma_start(Y[bass.ds(b * SLOTS + NE * SLOTS, SLOTS), n * 512:(n + 1) * 512],
                                          ysb[64 * n:64 * n + 64, 0, :]).then_inc(S[f"ov_out{l}"], 16)
                        act.wait_ge(S[f"ov_out{l}"], b * 32 + 32)
                        act.sem_inc(S["ov_turns_act"], 1)
                    act.end_ifs()
                act.sem_inc(S["moe_done_gather"], 1)

            def router(l):
                act.wait_ge(S["gexp_in"], l + 1)
                nc.scalar.activation(view(W, RB + 450, 12), view(W, RB + 450, 12), ACT.Exp).then_inc(S["gexp_out"], 1)
                act.wait_ge(S["eexp_in"], l + 1)
                nc.scalar.activation(view(W, RB + 470, 3), view(W, RB + 470, 3), ACT.Exp).then_inc(S["eexp_out"], 1)

            act.wait_ge(S["late_in"], LATE * 16)
            rms(0)
            broadcasts(0, 12)
            evac_h(0, hT, False)
            for t in range(NT):
                base = 4 * (t > 0)
                if t < 2:
                    act.wait_ge(S["z_in_psum"], t + 1)
                else:
                    act.wait_ge(S["units_used"], U_WIN0 + KD)
                    act.wait_ge(S["a_ready"], 1)
                nc.scalar.activation(ua[:, t % 2, :], ps[:, base, :], ACT.Gelu_apprx_tanh)
                nc.scalar.activation(va[:, t % 2, :], ps[:, base + 1, :], ACT.Gelu_apprx_tanh)
                if t:
                    act.wait_ge(S["sums_ready"], t)
                nc.scalar.activation(sq0[:, 0:512], ps[:, base + 2, :], ACT.Square, scale=HD ** -0.5)
                nc.scalar.activation(sq0[:, 512:640], ps[:, base + 3, 0:P], ACT.Square, scale=HD ** -0.5)
                nc.scalar.copy(v0[:, 0 if t == 0 else t + 1, :], ps[:, base + 3, P:2 * P])\
                    .then_inc(S["z_act_done"], 1)
                if t == 0:
                    act.wait_ge(S["z_act_done"], 1)
                    act.dma_start(O[3].rearrange("a s h d -> (a s) (h d)"), v0[:, 0, :]).then_inc(S["v_out"], 16)
                act.wait_ge(S["sums_ready"], t + 1)
                nc.scalar.activation(ss[:, 20:31], ss[:, 8:19], ACT.Sqrt, bias=eps[:, :]).then_inc(S["roots_ready"], 1)
                act.wait_ge(S["qkT_in_psum"], t + 1)
                nc.scalar.copy(qT0[:, t, :, :], ps[:, 1, :].rearrange("p (i q) -> p i q", i=4))
                nc.scalar.copy(kT0[:, 0 if t == 0 else t + 1, :], ps[:, 2, 0:P]).then_inc(S["qkT_ready"], 1)
            attention(0, batches(0))
            for n in range(NT):
                evac_cat(n)
            rms(1)
            broadcasts(12, 12)
            evac_h(1, h2T, True)
            router(0)
            experts(0)
            overflow(0)

            rms(2)
            act.dma_start(ckvc[:, :], A["cache_l1_ckv"].rearrange("a s d -> (a s) d")).then_inc(S["cache_in"], 16)
            act.dma_start(kpe[:, 3, :], A["cache_l1_kpe"].rearrange("a s d -> (a s) d")).then_inc(S["cache_in"], 16)
            broadcasts(24, 12)
            evac_h(2, hT, False)
            for t in range(NT):
                if t < 2:
                    act.wait_ge(S["z1_in_psum"], t + 1)
                else:
                    act.wait_ge(S["units_used"], U_WIN1 + 3)
                link(nc.scalar.activation(junk[:, 0:Q_LORA], ps[:, 2 * t, 0:Q_LORA], ACT.Square,
                                          scale=Q_LORA ** -0.5, accum_out=ss[:, t:t + 1]))
                link(nc.scalar.activation(junk[:, 0:KV_LORA], ps[:, 2 * t + 1, 0:KV_LORA], ACT.Square,
                                          scale=KV_LORA ** -0.5, accum_out=ss[:, 3 + t:4 + t]))
                link(nc.scalar.activation(junk[:, 0:ROPE], ps[:, 2 * t + 1, KV_LORA:KV_LORA + ROPE], ACT.Square,
                                          scale=QK ** -0.5, accum_out=ss[:, 32 + t:33 + t]))
                link(nc.scalar.copy(kpe[:, t, :], ps[:, 2 * t + 1, KV_LORA:KV_LORA + ROPE]))
            act.wait_ge(S["cache_in"], 32)
            link(nc.scalar.activation(junk[:, 0:ROPE], kpe[:, 3, :], ACT.Square,
                                      scale=QK ** -0.5, accum_out=ss[:, 35:36]))
            act.dma_start(O[5].rearrange("a s d -> (a s) d"), kpe[:, 0, :]).then_inc(S["v_out"], 16)
            nc.scalar.activation(ss[:, 8:14], ss[:, 0:6], ACT.Sqrt, bias=eps[:, :]).then_inc(S["z1_roots"], 1)
            for n, t in enumerate((3, 0, 1, 2)):
                act.wait_ge(S["cqkvT_in_psum"], n + 1)
                if t < 3:
                    nc.scalar.copy(cqT[:, t, :, :], ps[:, 2 * t, 0:Q_LORA].rearrange("p (k q) -> p k q", k=3))
                nc.scalar.copy(ckvT[:, t, :, :],
                               ps[:, 2 * t + (t < 3), 0:KV_LORA].rearrange("p (k q) -> p k q", k=2))\
                    .then_inc(S["cqkvT_ready"], 1)

            def square_prep(n, prep):
                kind, s, hb, t, j = prep
                base = 2 * (n % 2)
                act.wait_ge(S["prep_in_psum"], n + 1)
                if n:
                    act.wait_ge(S["prep_sums"], n)
                else:
                    act.wait_ge(S["l1_out"], 16)
                if n == PREP_AT[2]:
                    act.wait_ge(S["x_updated"], x_after(3))
                if kind == "kv":
                    kv = ps[:, base:base + 2, :].rearrange("p b (h c) -> p (b h) c", c=NOPE * 2)
                    nc.scalar.activation(sq1[:, :, 0:NOPE], kv[:, :, 0:NOPE], ACT.Square, scale=QK ** -0.5)\
                        .then_inc(S["prep_squares"], 1)
                    link(nc.scalar.copy(v1[:, j, :, :], kv[:, :, NOPE:]))
                else:
                    nc.scalar.activation(sq1[:, :, :].rearrange("p (b h) c -> p b (h c)", b=2),
                                         ps[:, base:base + 2, 0:384], ACT.Square, scale=QK ** -0.5)\
                        .then_inc(S["prep_squares"], 1)
                act.wait_ge(S["prep_sums"], n + 1)
                nc.scalar.activation(ss[:, 48:56], ss[:, 40:48], ACT.Sqrt, bias=eps[:, :])\
                    .then_inc(S["prep_roots"], 1)

            def evac_prep(n, prep):
                kind, s, hb, t, j = prep
                act.wait_ge(S["prepT_in_psum"], n + 1)
                src = ps[0:QK, 4 + 2 * (n % 2), :].rearrange("p (h q) -> p h q", h=4)
                dst = kT1[0:QK, 0:4, j, :] if kind == "kv" else qT1[0:QK, 0:4, :]
                nc.scalar.copy(dst, src).then_inc(S["prepT_act"], 1)

            for sweep, preps in enumerate(PREPS):
                at = PREP_AT[sweep]
                for n, prep in enumerate(preps):
                    square_prep(at + n, prep)
                    if n:
                        evac_prep(at + n - 1, preps[n - 1])
                evac_prep(at + len(preps) - 1, preps[-1])
                attention(1, batches(1, sweep))
                if sweep == 1:
                    evac_cat(3)
            evac_cat(4)
            evac_cat(5)
            rms(3)
            broadcasts(36, 12)
            evac_h(3, h2T, True)
            router(1)
            experts(1)
            overflow(1)
            act.wait_ge(S["x_updated"], 12)
            act.dma_start(O[0].rearrange("a s d -> (a s) d"), x[:, 0, :]).then_inc(S["out_done"], 16)
            act.dma_start(O[1].rearrange("a (t s) d -> s (a t) d", t=2), x[:, 1:3, :]).then_inc(S["out_done"], 16)
            act.wait_ge(S["out_done"], 2 * 16)
            act.wait_ge(S["k_out"], 16)
            act.wait_ge(S["l1_out"], 16)

        @block.vector
        def _(dve):
            V = nc.vector
            chain = [0]

            def link(ins):
                chain[0] += 1
                ins.then_inc(S["dve_chain"], 1)
                dve.wait_ge(S["dve_chain"], chain[0])

            def modulation(l, r):
                dve.wait_ge(S["units_used"], U_ADA[l] + (r + 1) * KD)
                row = m[:, l, r, :]
                if r == 1:
                    V.tensor_tensor(row, ps[:, 7, :], row, ALU.add).then_inc(S["m_ready"], 1)
                    return
                link(V.tensor_tensor(row, ps[:, 7, :], row, ALU.add))
                half = slice(64, 128) if r == 0 else slice(0, 64)
                V.scalar_tensor_tensor(out=m[half, l, r, :], in0=m[half, l, r, :], scalar=1.0,
                                       in1=gn[half, l, :], op0=ALU.add, op1=ALU.mult).then_inc(S["m_ready"], 1)

            def norm(stage):
                l, second = divmod(stage, 2)
                dve.wait_ge(S["rms_ready"], stage + 1)
                link(V.reciprocal(ss[:, 8:11], ss[:, 4:7]))
                dve.wait_ge(S["bc_ready"], 24 * l + 12 * second + 8)
                for t in range(NT):
                    c = cond_of(t)
                    a, b = AB[:, c * D:(c + 1) * D], AB[:, (2 + c) * D:(3 + c) * D]
                    mid = hmod[:, :] if second else h3[:, t, :]
                    link(V.scalar_tensor_tensor(out=mid, in0=x[:, t, :], scalar=ss[:, 8 + t:9 + t], in1=a,
                                                op0=ALU.mult, op1=ALU.mult))
                    if second:
                        V.tensor_tensor(hp[:, t, :, :].rearrange("p k q -> p q k"),
                                        mid.rearrange("p (q k) -> p q k", k=KD),
                                        b.rearrange("p (q k) -> p q k", k=KD), ALU.add).then_inc(S["h_ready"], 1)
                        dve.wait_ge(S["h_ready"], 3 * stage + t + 1)
                    else:
                        V.tensor_tensor(mid, mid, b, ALU.add).then_inc(S["h_ready"], 1)

            def evac_h(stage, dst, dbuf):
                for t in range(NT):
                    dve.wait_ge(S["hT_in_psum"], 3 * stage + t + 1)
                    if dbuf and t == 2:
                        dve.wait_ge(S["logits_in_psum"], 3 * (stage // 2) + 1)
                    V.tensor_copy(dst[:, t % 2 if dbuf else t, 4:8, :],
                                  ps[:, 2 * t + 1, :].rearrange("p (k q) -> p k q", k=4)).then_inc(S["hT_dve"], 1)

            def rope(xs, tmps, col, rot, heads):
                cos = over(con[:, col:col + rot], 1, [P, heads, rot])
                sin = con[:, col + rot:col + 2 * rot]
                for n in range(2):
                    link(V.tensor_tensor(tmps[:, :, n::2], xs[:, :, 1 - n::2],
                                         over(sin[:, n::2], 1, [P, heads, rot // 2]), ALU.mult))
                link(V.tensor_tensor(xs, xs, cos, ALU.mult))
                return V.tensor_tensor(xs, xs, tmps, ALU.add)

            def maxima(l, b):
                gb, t, i = b
                par = gb % 2
                nk = P if t == 0 else 384
                s = ps[:, 2 * par:2 * par + 2, 0:nk]
                dve.wait_ge(S["scores_in_psum"], gb + 1)
                if l == 0 and t:
                    at = 2 * P if t == 1 else P
                    part = ps[:, 2 * par:2 * par + 2, at:at + P]
                    mask = con[:, C_MASK + (t - 1) * P:C_MASK + t * P]
                    link(V.tensor_tensor(part, part, over(mask, 1, [P, 2, P]), ALU.add))
                link(V.tensor_reduce(st[:, gb % 4, 0:2], s, AX, ALU.max))
                if l == 0:
                    sk = sink[:, i:i + 5:4]
                    link(V.scalar_tensor_tensor(out=st[:, gb % 4, 2:4], in0=st[:, gb % 4, 0:2], scalar=HD ** -0.5,
                                                in1=sk, op0=ALU.mult, op1=ALU.max))
                    link(V.tensor_tensor(st[:, gb % 4, 6:8], sk, st[:, gb % 4, 2:4], ALU.subtract))
                    V.tensor_scalar(st[:, gb % 4, 4:6], st[:, gb % 4, 2:4], -1.0, None, ALU.mult)\
                        .then_inc(S["max_ready"], 1)
                else:
                    V.tensor_scalar(st[:, gb % 4, 4:6], st[:, gb % 4, 0:2], -QK ** -0.5, None, ALU.mult)\
                        .then_inc(S["max_ready"], 1)

            def evac_pT(l, b):
                gb, t, i = b
                par = gb % 2
                pT = (pT0, pT1)[l]
                dve.wait_ge(S["pT_in_psum"], gb + 1)
                if gb >= 2:
                    dve.wait_ge(S["att_in_psum"], gb - 1)
                if t == 0:
                    V.tensor_copy(pT[:, par, 0, P:2 * P], ps[:, 5, 0:P]).then_inc(S["pT_dve"], 1)
                else:
                    V.tensor_copy(pT[:, par, 2, :], ps[:, 5, 0:2 * P]).then_inc(S["pT_dve"], 1)

            def normalize(l, b):
                gb, t, i = b
                par = gb % 2
                dve.wait_ge(S["att_in_psum"], gb + 1)
                den = st[:, gb % 4, 10:12]
                if l == 0:
                    link(V.tensor_tensor(den, den, st[:, gb % 4, 8:10], ALU.add))
                link(V.reciprocal(st[:, gb % 4, 12:14], den))
                r = over(st[:, gb % 4, 12:14], 2, [P, 2, HD])
                if l == 0:
                    dst = cat0[:, t, 512:1024].rearrange("p (v i d) -> p v i d", v=2, i=4)[:, :, i, :]
                else:
                    sweep = (gb - len(MIX0)) // 4
                    at = SWEEPS[sweep][1] * 512 + i * P
                    dst = cat1[:, max(t - 1, 0), at:at + P].rearrange("p (v d) -> p v d", v=2)
                V.tensor_tensor(dst, ps[:, 6, 0:P].rearrange("p (v d) -> p v d", v=2), r, ALU.mult)\
                    .then_inc(S["att_ready"], 1)

            def attention(l, todo):
                maxima(l, todo[0])
                for n, b in enumerate(todo):
                    if n + 1 < len(todo):
                        maxima(l, todo[n + 1])
                    evac_pT(l, b)
                    if n:
                        normalize(l, todo[n - 1])
                normalize(l, todo[-1])

            def residual(n, t, last_of_layer):
                if n == 0:
                    dve.wait_ge(S["fill_done"], 1)
                dve.wait_ge(S["catT_in_psum"], n + 1)
                if n >= 2:
                    dve.wait_ge(S["x_updated"], x_after(n - 2))
                V.tensor_copy(catT[:, n % 2, 4:8, :],
                              ps[:, 2 * (n % 2) + 1, :].rearrange("p (k q) -> p k q", k=4))\
                    .then_inc(S["catT_dve"], 1)
                if last_of_layer is None:
                    dve.wait_ge(S["y_in_psum"], (1, 2, None, 3, 4)[n])
                else:
                    dve.wait_ge(S["units_used"], U_WO[last_of_layer] + 4)
                dve.wait_ge(S["bc_ready"], 24 * (n // 3) + 12)
                base = 4 + 2 * (n % 2)
                link(V.tensor_tensor(tmp, ps[:, base:base + 2, :].rearrange("p b n -> p (b n)"),
                                     G[:, cond_of(t), :], ALU.mult))
                V.tensor_tensor(x[:, t, :], x[:, t, :], tmp, ALU.add).then_inc(S["x_updated"], 1)
                dve.wait_ge(S["x_updated"], x_after(n))

            def first_max(src, pri, key, top, mask, n):
                link(V.tensor_reduce(top, src, AX, ALU.max))
                link(V.tensor_tensor(key, src, over(top, 2, [P, NT, n]), ALU.is_equal))
                link(V.tensor_tensor(key, key, over(pri, 1, [P, NT, n]), ALU.mult))
                link(V.tensor_reduce(ss[:, 60:63], key, AX, ALU.max))
                link(V.tensor_tensor(mask, key, over(ss[:, 60:63], 2, [P, NT, n]), ALU.is_equal))

            def router(l):
                at = [RB]

                def new(*shape):
                    at[0] += math.prod(shape)
                    return view(W, at[0] - math.prod(shape), *shape)

                picks = new(NT, NE)
                lg = new(NT, NG + NE)
                gmask = new(NT, NG)
                masks = [new(NT, EPG), new(NT, EPG)]
                at[0] = RB + 300
                spread = new(P)
                at[0] = RB + 450
                gexp = new(NT, NG)
                at[0] = RB + 470
                e21 = new(NT)
                key = new(NT, EPG)
                le = new(NT, EPG)
                top = [new(NT), new(NT), new(NT)]
                pg = new(NT)
                wk = new(NT, 2)
                wide = new(NT, NE)
                pick2 = [new(NT, NE), new(NT, NE)]
                rank = new(NT, NE)
                cnt = new(NE)
                nover = new(NE)
                ofs = new(NE)
                jumps = new(NT, NE)
                blk = new(NT, NE)
                mod = new(NT, NE)
                blks = new(2, NT)
                mods = new(2, NT)
                hit = new(NT, NB)
                obs = new(OVER, NE)
                obs2 = new(OVER, NE)
                obe = new(OVER)
                assert at[0] <= 10 * D
                lgg, lge = lg[:, :, 0:NG], lg[:, :, NG:]

                dve.wait_ge(S["logits_in_psum"], 3 * (l + 1))
                dve.wait_ge(S["v_out"], 16 * (l + 1))
                link(V.tensor_tensor(lg, ps[:, 6, 0:NT * 36].rearrange("p (t n) -> p t n", t=NT),
                                     over(br[:, l, :], 1, [P, NT, NG + NE]), ALU.add))
                first_max(lgg, con[:, C_PRI4:C_PRI4 + NG], key[:, :, 0:NG], top[0], gmask, NG)
                V.tensor_tensor(gexp, lgg, over(top[0], 2, [P, NT, NG]), ALU.subtract).then_inc(S["gexp_in"], 1)
                for t in range(NT):
                    last = V.tensor_tensor(wide[:, t, :].rearrange("p (g e) -> p g e", g=NG),
                                           lge[:, t, :].rearrange("p (g e) -> p g e", g=NG),
                                           over(gmask[:, t, :], 2, [P, NG, EPG]), ALU.mult)
                link(last)
                link(V.tensor_reduce(le, wide.rearrange("p t (g e) -> p t e g", g=NG), AX, ALU.add))
                first_max(le, con[:, C_PRI8:C_PRI8 + EPG], key, top[1], masks[0], EPG)
                link(V.scalar_tensor_tensor(out=le, in0=masks[0], scalar=NEG, in1=le, op0=ALU.mult, op1=ALU.add))
                first_max(le, con[:, C_PRI8:C_PRI8 + EPG], key, top[2], masks[1], EPG)
                V.tensor_tensor(e21, top[2], top[1], ALU.subtract).then_inc(S["eexp_in"], 1)
                for k in range(2):
                    for t in range(NT):
                        last = V.tensor_tensor(pick2[k][:, t, :].rearrange("p (g e) -> p g e", g=NG),
                                               over(gmask[:, t, :], 2, [P, NG, EPG]),
                                               over(masks[k][:, t, :], 1, [P, NG, EPG]), ALU.mult)
                link(last)
                V.tensor_tensor(picks, pick2[0], pick2[1], ALU.add).then_inc(S["picks_ready"], 1)
                dve.wait_ge(S["gexp_out"], l + 1)
                link(V.tensor_reduce(pg, gexp, AX, ALU.add))
                link(V.reciprocal(pg, pg))
                dve.wait_ge(S["eexp_out"], l + 1)
                link(V.tensor_scalar(wk[:, :, 0], e21, 1.0, None, ALU.add))
                link(V.reciprocal(wk[:, :, 0], wk[:, :, 0]))
                link(V.tensor_tensor(wk[:, :, 1], e21, wk[:, :, 0], ALU.mult))
                link(V.tensor_tensor(gates[:, :, :], wk, over(pg, 2, [P, NT, 2]), ALU.mult))
                dve.wait_ge(S["rank_in_psum"], l + 1)
                link(V.tensor_copy(rank, ps[:, 7, 0:NT * NE].rearrange("p (t n) -> p t n", t=NT)))
                link(V.tensor_copy(cnt, ps[:, 7, NT * NE:(NT + 1) * NE]))
                link(V.tensor_scalar(nover, cnt, float(SLOTS), None, ALU.is_gt))
                for n in range(2, MAX_BLOCKS):
                    link(V.scalar_tensor_tensor(out=nover, in0=cnt, scalar=float(SLOTS * n), in1=nover,
                                                op0=ALU.is_gt, op1=ALU.add))
                link(V.tensor_tensor(wide[:, 0, :], nover, con[:, C_ID:C_ID + NE], ALU.mult))
                link(V.tensor_reduce(ss[:, 63:64], wide[:, 0, :], AX, ALU.add))
                V.tensor_scalar(spread, ones[:, :], ss[:, 63:64], None, ALU.mult).then_inc(S["nover_ready"], 1)
                link(V.tensor_scalar(jumps, rank, float(SLOTS), None, ALU.is_ge))
                link(V.tensor_copy(blk, jumps))
                for n in range(2, MAX_BLOCKS):
                    link(V.scalar_tensor_tensor(out=jumps, in0=rank, scalar=float(SLOTS * n), in1=jumps,
                                                op0=ALU.is_ge, op1=ALU.add))
                link(V.scalar_tensor_tensor(out=mod, in0=jumps, scalar=-float(SLOTS), in1=rank,
                                            op0=ALU.mult, op1=ALU.add))
                dve.wait_ge(S["ofs_in_psum"], l + 1)
                link(V.tensor_copy(ofs, ps[:, 6, 0:NE]))
                link(V.tensor_tensor(wide[:, 0, :], ofs, con[:, C_31:C_31 + NE], ALU.add))
                link(V.tensor_tensor(blk, blk, over(wide[:, 0, :], 1, [P, NT, NE]), ALU.mult))
                link(V.tensor_tensor(blk, blk, jumps, ALU.add))
                link(V.tensor_tensor(blk, blk, over(iota[:, 0:NE], 1, [P, NT, NE]), ALU.add))
                for k in range(2):
                    for src, dst in ((blk, blks), (mod, mods)):
                        link(V.tensor_tensor(wide, pick2[k], src, ALU.mult))
                        link(V.tensor_reduce(dst[:, k, :], wide, AX, ALU.add))
                link(V.scalar_tensor_tensor(out=tabi[:, l, :].rearrange("p (k t) -> p k t", k=2), in0=blks,
                                            scalar=float(SLOTS), in1=mods, op0=ALU.mult, op1=ALU.add))
                link(V.tensor_scalar(mods, mods, 1.0, None, ALU.add))
                for k in range(2):
                    dst = slotm if k == 0 else hit
                    link(V.tensor_tensor(dst, over(iota[:, 0:NB], 1, [P, NT, NB]),
                                         over(blks[:, k, :], 2, [P, NT, NB]), ALU.is_equal))
                    link(V.tensor_tensor(dst, dst, over(mods[:, k, :], 2, [P, NT, NB]), ALU.mult))
                link(V.tensor_tensor(slotm, slotm, hit, ALU.add))
                link(V.tensor_scalar(slotm, slotm, -1.0, None, ALU.add))
                o1, n1 = ofs[0:1, :], nover[0:1, :]
                link(V.tensor_tensor(n1, n1, o1, ALU.add))
                bi = over(iota[0:1, 0:OVER], 2, [1, OVER, NE])
                link(V.tensor_tensor(obs[0:1], over(o1, 1, [1, OVER, NE]), bi, ALU.is_le))
                link(V.tensor_tensor(obs2[0:1], over(n1, 1, [1, OVER, NE]), bi, ALU.is_gt))
                link(V.tensor_tensor(obs[0:1], obs[0:1], obs2[0:1], ALU.mult))
                link(V.tensor_tensor(obs[0:1], obs[0:1], over(iota[0:1, 0:NE], 1, [1, OVER, NE]), ALU.mult))
                link(V.tensor_reduce(obe[0:1], obs[0:1], AX, ALU.add))
                link(V.tensor_copy(ovi[0:1, l, 0:OVER], obe[0:1]))
                V.tensor_copy(ovi[0:1, l, 15:16], n1[:, NE - 1:NE]).then_inc(S["route_ready"], 1)

            def one_hot(par, column, done):
                return V.tensor_tensor(rows[:, par, :, :], over(iota[:, 0:SLOTS], 1, [P, NT, SLOTS]),
                                       slotm[:, :, column].to_broadcast([P, NT, SLOTS]), ALU.is_equal)\
                    .then_inc(done, 1)

            def experts(l):
                link(V.memset(hh[0:64, :], 0.0))
                one_hot(0, slice(0, 1), S["rows_ready"])
                with dve.Fori(0, NE // 4) as i:
                    for u in range(4):
                        par = u % 2
                        e = i * 4 + u
                        dve.wait_ge(S["gathered"], e + (l * (NE + 1) + 1))
                        V.tensor_copy(xT[:, par, :, :], ps[:, par, :].rearrange("p (k s) -> p k s", k=KD))\
                            .then_inc(S["xT_ready"], 1)
                        one_hot(1 - par, bass.ds(e + 1, 1), S["rows_ready"])
                        dve.wait_ge(S["silu_ready"], e + (l * NE + 1))
                        V.tensor_tensor(hh[64:128, :], silu, ps[64:128, 2 + par, 0:DE], ALU.mult).then_inc(S["hh_ready"], 1)

            def overflow(l):
                count = dve.value_load(ovi[0:1, l, 15:16], min_val=0, max_val=OVER)
                dve.wait_ge(S["gathered"], (l + 1) * (NE + 1))
                with dve.Fori(0, OVER) as b:
                    with dve.If(b < count):
                        one_hot(0, bass.ds(b + NE, 1), S[f"ov_rows{l}"])
                        dve.wait_ge(S[f"ov_gathered{l}"], b + 1)
                        V.tensor_copy(xT[:, 0, :, :], ps[:, 0, :].rearrange("p (k s) -> p k s", k=KD))\
                            .then_inc(S[f"ov_xT{l}"], 1)
                        dve.wait_ge(S[f"ov_silu{l}"], b + 1)
                        V.tensor_tensor(hh[64:128, :], silu, ps[64:128, 2, 0:DE], ALU.mult).then_inc(S[f"ov_hh{l}"], 1)
                    dve.end_ifs()

            def combine(l):
                for t in range(NT):
                    for k in range(2):
                        dve.wait_ge(S[f"pair_rows{2 * t + k}"], 16 * (l + 1))
                    p0, p1 = pair[:, 2 * (t % 2), :], pair[:, 2 * (t % 2) + 1, :]
                    link(V.tensor_scalar(p0, p0, gates[:, t, 0:1], None, ALU.mult))
                    link(V.scalar_tensor_tensor(out=p0, in0=p1, scalar=gates[:, t, 1:2], in1=p0,
                                                op0=ALU.mult, op1=ALU.add))
                    dve.wait_ge(S["bc_ready"], 24 * (l + 1))
                    link(V.tensor_tensor(p0, p0, G[:, cond_of(t), :], ALU.mult))
                    V.tensor_tensor(x[:, t, :], x[:, t, :], p0, ALU.add).then_inc(S["x_updated"], 1)
                dve.wait_ge(S["x_updated"], 6 * (l + 1))

            V.memset(m[:, :, :, :], 0.0)
            V.memset(gn[:, :, :], 0.0).then_inc(S["tiles_cleared"], 1)
            V.memset(scT[:, :, :], 0.0)
            V.memset(eps[:, :], EPS)
            V.memset(ones[:, :], 1.0).then_inc(S["tiles_cleared"], 1)
            dve.wait_ge(S["early_in"], EARLY * 16)
            for r in range(3):
                modulation(0, r)
            dve.wait_ge(S["late_in"], LATE * 16)
            norm(0)
            evac_h(0, hT, False)
            for t in range(NT):
                base = 4 * (t > 0)
                dve.wait_ge(S["z_act_done"], t + 1)
                link(V.bn_stats(ss[:, 32:38], va[:, t % 2, :]))
                link(V.bn_aggr(ss[:, 38:40], ss[:, 32:38]))
                link(V.tensor_copy(ss[:, 18:19], ss[:, 39:40]))
                V.tensor_reduce(ss[:, 8:18], sq0.rearrange("p (h d) -> p h d", h=B_HEADS + 2), AX, ALU.add)\
                    .then_inc(S["sums_ready"], 1)
                dve.wait_ge(S["roots_ready"], t + 1)
                link(V.reciprocal(ss[:, 44:55], ss[:, 20:31]))
                v = va[:, t % 2, :]
                link(V.tensor_scalar(v, v, ss[:, 38:39], ss[:, 54:55], ALU.subtract, ALU.mult))
                V.tensor_tensor(v, v, gvn[:, :], ALU.mult).then_inc(S["v_ready"], 1)
                if t:
                    dve.wait_ge(S["qkT_in_psum"], t)
                if t == 1:
                    dve.wait_ge(S["k_out"], 16)
                for kv in range(2):
                    V.tensor_tensor(qk[:, 0:512].rearrange("p (i v d) -> p i v d", i=4, v=2)[:, :, kv, :],
                                    ps[:, base + 2, kv * 256:(kv + 1) * 256].rearrange("p (i d) -> p i d", i=4),
                                    over(ss[:, 44 + 4 * kv:48 + 4 * kv], 2, [P, 4, HD]), ALU.mult)
                link(V.tensor_tensor(qk[:, 512:640].rearrange("p (v d) -> p v d", v=2),
                                     ps[:, base + 3, 0:P].rearrange("p (v d) -> p v d", v=2),
                                     over(ss[:, 52:54], 2, [P, 2, HD]), ALU.mult))
                heads = qk.rearrange("p (h d) -> p h d", d=HD)
                if t == 0:
                    V.tensor_tensor(qk, qk, gqk[:, :], ALU.mult).then_inc(S["qk_ready"], 1)
                else:
                    link(V.tensor_tensor(qk, qk, gqk[:, :], ALU.mult))
                    rope(heads, rt0.rearrange("p (h d) -> p h d", d=HD), C_R0 + (t - 1) * 2 * HD, HD,
                         B_HEADS + 2).then_inc(S["qk_ready"], 1)
                dve.wait_ge(S["mixed_in_psum"], t + 1)
                for g in range(A_GROUPS):
                    part = slice(g * P, (g + 1) * P)
                    last = V.scalar_tensor_tensor(out=cat0[:, t, part], in0=ps[:, 0, part],
                                                  scalar=bsT[:, g:g + 1], in1=ua[:, t % 2, part],
                                                  op0=ALU.add, op1=ALU.mult)
                last.then_inc(S["a_ready"], 1)
            todo = batches(0)
            maxima(0, todo[0])
            for n, b in enumerate(todo):
                if n + 1 < len(todo):
                    maxima(0, todo[n + 1])
                evac_pT(0, b)
                if n:
                    normalize(0, todo[n - 1])
                if n % 4 == 3:
                    modulation(1, n // 4)
            normalize(0, todo[-1])
            for t in range(NT):
                residual(t, t, 0 if t == 2 else None)
            norm(1)
            evac_h(1, h2T, True)
            router(0)
            dve.wait_ge(S["route_ready"], 1)
            experts(0)
            overflow(0)
            combine(0)

            norm(2)
            evac_h(2, hT, False)
            dve.wait_ge(S["z1_roots"], 1)
            link(V.reciprocal(ss[:, 16:22], ss[:, 8:14]))
            for t in range(NT):
                V.scalar_tensor_tensor(out=cqn[:, t, :], in0=ps[:, 2 * t, 0:Q_LORA], scalar=ss[:, 16 + t:17 + t],
                                       in1=gqa[:, :], op0=ALU.mult, op1=ALU.mult)
                V.scalar_tensor_tensor(out=ckvn[:, t, :], in0=ps[:, 2 * t + 1, 0:KV_LORA],
                                       scalar=ss[:, 19 + t:20 + t], in1=gkva[:, :], op0=ALU.mult,
                                       op1=ALU.mult).then_inc(S["cqkv_ready"], 1)

            def prep(n, p):
                kind, s, hb, t, j = p
                base = 2 * (n % 2)
                width = NOPE if kind == "kv" else QK
                dve.wait_ge(S["prep_squares"], n + 1)
                red = V.tensor_reduce(ss[:, 40:48], sq1[:, :, 0:width], AX, ALU.add)
                if kind == "kv":
                    link(red)
                    V.tensor_scalar(ss[:, 40:48], ss[:, 40:48], ss[:, 32 + t:33 + t], None, ALU.add)\
                        .then_inc(S["prep_sums"], 1)
                else:
                    red.then_inc(S["prep_sums"], 1)
                dve.wait_ge(S["prep_roots"], n + 1)
                if n:
                    dve.wait_ge(S["prepT_in_psum"], n)
                else:
                    dve.wait_ge(S["cqkvT_in_psum"], 4)
                    dve.wait_ge(S["l1_out"], 16)
                link(V.reciprocal(ss[:, 56:64], ss[:, 48:56]))
                rn = ss[:, 56:64]
                if kind == "kv":
                    kv = ps[:, base:base + 2, :].rearrange("p b (h c) -> p (b h) c", c=2 * NOPE)
                    V.tensor_tensor(kw[:, :, 0:NOPE], kv[:, :, 0:NOPE], over(rn, 2, [P, HALF, NOPE]), ALU.mult)
                    link(V.tensor_tensor(kw[:, :, NOPE:], over(kpe[:, t, :], 1, [P, HALF, ROPE]),
                                         over(rn, 2, [P, HALF, ROPE]), ALU.mult))
                else:
                    for q in range(2):
                        last = V.tensor_tensor(kw[:, 4 * q:4 * q + 4, :],
                                               ps[:, base + q, 0:384].rearrange("p (h c) -> p h c", c=QK),
                                               over(rn[:, 4 * q:4 * q + 4], 2, [P, 4, QK]), ALU.mult)
                    link(last)
                gain = over((gk1 if kind == "kv" else gq1)[:, :], 1, [P, HALF, QK])
                if t in (0, 3):
                    V.tensor_tensor(kw, kw, gain, ALU.mult).then_inc(S["prep_ready"], 1)
                else:
                    link(V.tensor_tensor(kw, kw, gain, ALU.mult))
                    rope(kw[:, :, NOPE:], rt1, C_R1 + (t - 1) * 2 * ROPE, ROPE, HALF).then_inc(S["prep_ready"], 1)

            def evac_prep(n, p):
                kind, s, hb, t, j = p
                dve.wait_ge(S["prepT_in_psum"], n + 1)
                src = ps[0:QK, 5 + 2 * (n % 2), :].rearrange("p (h q) -> p h q", h=4)
                dst = kT1[0:QK, 4:8, j, :] if kind == "kv" else qT1[0:QK, 4:8, :]
                V.tensor_copy(dst, src).then_inc(S["prepT_dve"], 1)

            for sweep, preps in enumerate(PREPS):
                at = PREP_AT[sweep]
                for n, p in enumerate(preps):
                    prep(at + n, p)
                    if n:
                        evac_prep(at + n - 1, preps[n - 1])
                evac_prep(at + len(preps) - 1, preps[-1])
                attention(1, batches(1, sweep))
                if sweep == 1:
                    residual(3, 0, None)
            residual(4, 1, None)
            residual(5, 2, 1)
            norm(3)
            evac_h(3, h2T, True)
            router(1)
            dve.wait_ge(S["route_ready"], 2)
            experts(1)
            overflow(1)
            combine(1)

        @block.gpsimd
        def _(pool):
            pool.sem_inc(S["y_evac"], 2)
            for par in range(2):
                pool.sem_inc(S[f"y_out{par}"], 32)
            pool.wait_ge(S["z_in_psum"], 1)
            for n in range(0, OVER * SLOTS, P):
                count = min(P, OVER * SLOTS - n)
                pool.dma_start(Y[NE * SLOTS + n:NE * SLOTS + n + count, :], x[0:count, 0, :])\
                    .then_inc(S["filled"], 16)
            pool.wait_ge(S["filled"], 16 * (-(-OVER * SLOTS // P)))
            pool.sem_inc(S["fill_done"], 1)
            for l in range(N_LAYERS):
                if l == 0:
                    pool.wait_ge(S["qk_ready"], 1)
                    pool.dma_start(O[2].rearrange("a s h d -> (a s) (h d)"), qk[:, 512:640]).then_inc(S["k_out"], 16)
                else:
                    pool.wait_ge(S["cqkv_ready"], 1)
                    pool.dma_start(O[4].rearrange("a s d -> (a s) d"), ckvn[:, 0, :]).then_inc(S["l1_out"], 16)
                pool.wait_ge(S["route_ready"], l + 1)
                pool.wait_ge(S["moe_done_gather"], l + 1)
                pool.wait_ge(S["gathered"], (l + 1) * (NE + 1))
                for t in range(NT):
                    for k in range(2):
                        if t == 2:
                            pool.wait_ge(S["x_updated"], 6 * l + 4)
                        dst = pair[:, 2 * (t % 2) + k, :]
                        idx = bass.IndirectOffsetOnAxis(tabi[:, l, 3 * k + t:3 * k + t + 1], 0)
                        done = S[f"pair_rows{2 * t + k}"]
                        pool.indirect_dma_start(dst, None, Y[:, :], idx).then_inc(done, 16)


def x_after(n):
    return n + 1 if n < 3 else n + 4


EARLY = 3 + N_LAYERS * 8
LATE = 6 + (B_HEADS + 2) + 6 + 4 * N_LAYERS


_CONSTS = "shape_constants"
_OUTS = [(1, P, D), (1, 2 * P, D), (1, P, 2, HD), (1, P, 2, HD), (1, P, KV_LORA), (1, P, ROPE)]


def kernel(**inputs):
    import concourse.bacc as bacc
    from concourse.bass_utils import run_bass_kernel_spmd

    nc = bacc.Bacc("TRN2", target_bir_lowering=False, num_devices=1)
    arrays = {"in_" + k: np.ascontiguousarray(v) for k, v in inputs.items()}
    arrays["in_" + _CONSTS] = shape_constants()
    A = {k[3:]: nc.dram_tensor(k, v.shape, mybir.dt.from_np(v.dtype), kind="ExternalInput").ap()
         for k, v in arrays.items()}
    O = [nc.dram_tensor(f"out_{i}", s, mybir.dt.float32, kind="ExternalOutput").ap() for i, s in enumerate(_OUTS)]
    Y = nc.dram_tensor("expert_rows", ((NE + OVER) * SLOTS, D), mybir.dt.float32).ap()
    trunk(nc, A, O, Y)
    r = run_bass_kernel_spmd(nc, [arrays], core_ids=[0])
    return tuple(r.results[0][f"out_{i}"] for i in range(len(_OUTS)))
```

```python
import math
from contextlib import ExitStack

import numpy as np
import concourse.bass as bass
from concourse import mybir

P = 128
D = 1024
KD = D // P
NT = 3
N_LAYERS = 2
EPS = 1e-6
NEG = -1e30
A_WIDTH = 512
A_GROUPS = 4
HD = 64
B_HEADS = 8
QKW = (B_HEADS + 2) * HD
EVEN_IN = 2 * A_WIDTH + QKW + 2 * HD
C_HEADS = 16
HALF = C_HEADS // 2
QK = 96
NOPE = 64
ROPE = 32
Q_LORA = 384
KV_LORA = 256
ODD_IN = Q_LORA + KV_LORA + ROPE
NG = 4
EPG = 8
NE = NG * EPG
DE = 256
SLOTS = 64
MAX_BLOCKS = NT * P // SLOTS
OVER = (2 * NT * P) // (SLOTS + 1)
NB = NE + 1 + OVER
RING = 12
SLOT = 2048

U_ADA = ((0, 12, 24), (32, 40, 48))
U_WIN_UV = 8
U_WIN_QK = 20
U_WO = (56, 164)
U_MOE = (60, 168)
U_WIN1 = 156
U_UQ = 159
U_UKV = 162
UV = 2 * A_WIDTH
QKV = EVEN_IN - UV


def used(unit):
    return unit + 1 if unit < U_MOE[0] else unit + 1 - 3 * NE


C_ID, C_TRI, C_SEL, C_MASK, C_R0, C_R1, C_IOTA, C_PRI8, C_PRI4, C_31 = (
    0, 128, 256, 512, 768, 1024, 1152, 1216, 1224, 1228)
C_N = 1260


def shape_constants():
    c = np.zeros((P, C_N), np.float32)
    i = np.arange(P)
    c[:, C_ID:C_ID + P] = np.eye(P)
    c[:, C_TRI:C_TRI + P] = i[:, None] < i[None, :]
    for cond in range(2):
        c[:, C_SEL + cond * P:C_SEL + (cond + 1) * P] = (i % 32 == cond)[:, None]
    c[:, C_MASK:C_MASK + P] = np.where(i[None, :] <= i[:, None], 0.0, NEG)
    c[:, C_MASK + P:C_MASK + 2 * P] = np.where(i[:, None] <= i[None, :], 0.0, NEG)
    for col, rot in ((C_R0, HD), (C_R1, ROPE)):
        half = rot // 2
        inv = np.float32(10000.0) ** (-np.arange(0, half, 2, dtype=np.float32) / np.float32(half))
        n = np.arange(2 * P)
        ang = np.concatenate([(n // 64).astype(np.float32)[:, None] * inv,
                              (n % 64).astype(np.float32)[:, None] * inv], -1).astype(np.float32)
        cos, sin = np.cos(ang), np.sin(ang)
        for t in range(2):
            at = col + t * 2 * rot
            c[:, at:at + rot] = np.repeat(cos[t * P:(t + 1) * P], 2, axis=1)
            c[:, at + rot:at + 2 * rot:2] = -sin[t * P:(t + 1) * P]
            c[:, at + rot + 1:at + 2 * rot:2] = sin[t * P:(t + 1) * P]
    c[:, C_IOTA:C_IOTA + 64] = np.arange(64)
    c[:, C_PRI8:C_PRI8 + EPG] = EPG - np.arange(EPG)
    c[:, C_PRI4:C_PRI4 + NG] = NG - np.arange(NG)
    c[:, C_31:C_31 + NE] = NE - 1 - np.arange(NE)
    return c


SEMS = """cond_in early_in late_in ov_turns_sp ov_turns_act filled fill_done v_out cache_in ring_full0 ring_full1 ring_full2 ring_full3 ring_full4 ring_full5
 ring_full6 ring_full7 ring_full8 ring_full9 ring_full10 ring_full11 units_used up_done down_done cond_ready
 tiles_cleared ws_in_psum ws_ready m_ready bc_in_psum bc_ready rms_ready h_ready hT_in_psum hT_act
 hT_dve z_act_done sums_ready gelu_done v_in var_ready var_roots kc_ready roots_ready v_ready qk_ready k_out mixed_in_psum a_ready
 qkT_in_psum qkT_ready kc_in_psum scores_in_psum max_ready probs_ready pT_in_psum pT_act pT_dve
 att_in_psum att_ready catT_in_psum catT_act catT_dve y_in_psum x_updated
 z1_in_psum z1_sums z1_roots cqkv_ready cqkvT_in_psum cqkvT_ready l1_out prep_in_psum prep_squares
 prep_sums prep_roots prep_ready prepT_in_psum prepT_act prepT_dve
 logits_in_psum gexp_in gexp_out eexp_in eexp_out picks_ready rank_in_psum nover_ready
 ofs_in_psum route_ready rows_ready gathered xT_ready silu_ready hh_ready hhT_in_psum
 hhT_ready y_evac y_out0 y_out1 moe_done_gather pair_rows0 pair_rows1 pair_rows2 pair_rows3 pair_rows4
 pair_rows5 pair_read out_done act_chain dve_chain
 ov_free0 ov_free1 ov_w0 ov_w1 ov_rows0 ov_rows1 ov_gathered0 ov_gathered1 ov_xT0 ov_xT1 ov_h0 ov_h1 ov_silu0 ov_silu1
 ov_hh0 ov_hh1 ov_hhT0 ov_hhT1 ov_hhTs0 ov_hhTs1 ov_y0 ov_y1 ov_evac0 ov_evac1 ov_out0 ov_out1""".split()


def trunk(nc, A, O, Y):
    f32, i32 = mybir.dt.float32, mybir.dt.int32
    ALU, ACT, AX = mybir.AluOpType, mybir.ActivationFunctionType, mybir.AxisListType.X
    ctx = ExitStack()
    with ctx:
        S = {name: ctx.enter_context(nc.semaphore(name)) for name in SEMS}
        ring_full = [S[f"ring_full{i}"] for i in range(RING)]

        def sb(name, *shape, dt=f32):
            return ctx.enter_context(nc.sbuf_tensor(name, [P, *shape], dt))

        ring = sb("ring", RING, SLOT)
        x = sb("x_tiles", NT, D)
        AB = sb("scale_shift", 4 * D)
        G = sb("gate_rows", 2, D)
        m = sb("modulation", N_LAYERS, 3, 512)
        gn = sb("norm_gains", N_LAYERS, 512)
        con = sb("constants", C_N)
        ones = sb("ones", P)
        gvn = sb("gvn", A_WIDTH)
        gqk = sb("gqk", QKW)
        wsT = sb("wsT", A_GROUPS, P)
        bsT = sb("bsT", A_GROUPS)
        sink = sb("sink", B_HEADS)
        gqa = sb("gqa", Q_LORA)
        gkva = sb("gkva", KV_LORA)
        gq1 = sb("gq1", QK)
        gk1 = sb("gk1", QK)
        wr = sb("wr", N_LAYERS, KD, NG + NE)
        br = sb("br", N_LAYERS, NG + NE)
        cT = sb("cT", 2, KD)
        scT = sb("scT", KD, 32)
        eps = sb("eps", 1)
        ss = sb("sums_of_squares", 64)
        st = sb("softmax_stats", 4, 16)
        W = sb("scratch", 10 * D)
        tabi = sb("pair_index", N_LAYERS, 6, dt=i32)
        ovi = sb("overflow_blocks", N_LAYERS, 16, dt=i32)
        gates = sb("gates", NT, 2)
        ps = ctx.enter_context(nc.psum_tensor("psum", [P, 8, 512], f32))

        ident = con[:, C_ID:C_ID + P]
        iota = con[:, C_IOTA:C_IOTA + 64]

        def view(tile, at, *shape):
            n = math.prod(shape)
            v = tile[:, at:at + n]
            if len(shape) == 1:
                return v
            names = "abc"[:len(shape)]
            return v.rearrange(f"p ({' '.join(names)}) -> p {' '.join(names)}",
                               **dict(zip(names[1:], shape[1:])))

        def over(ap, axis, shape):
            return ap.unsqueeze(axis).to_broadcast(shape)

        hT = view(W, 0, NT, KD, P)
        h3 = view(W, 3 * D, NT, D)
        cat0 = view(W, 3 * D, NT, D)
        ws = view(W, 6 * D, A_GROUPS, P)
        qT0 = view(W, 6 * D, NT, 4, P)
        kT0 = view(W, 7680, 4, P)
        v0 = view(W, 8192, 4, P)
        kc = view(W, 8704, P)
        ua = view(AB, 0, NT, A_WIDTH)
        va = view(AB, 1536, NT, A_WIDTH)
        qk = view(W, 8832, QKW)
        sq0 = view(AB, 3072, QKW)
        rt0 = sq0
        probs0 = view(W, 0, 2, 2, 384)
        pT0 = view(W, 1536, 2, 3, 256)
        kT1 = view(W, 0, HALF, 3, P)
        v1 = view(W, 3072, 3, HALF, NOPE)
        qT1 = view(W, 4608, HALF, P)
        cqT = view(W, 5632, NT, 3, P)
        ckvT = view(W, 6784, 4, 2, P)
        kpe = view(W, 7808, 4, ROPE)
        ckvc = view(W, 7936, KV_LORA)
        cat1 = view(W, 8192, 2, D)
        cqn = view(AB, 0, NT, Q_LORA)
        ckvn = view(AB, NT * Q_LORA, NT, KV_LORA)
        kw = view(AB, 0, HALF, QK)
        sq1 = view(AB, 768, HALF, QK)
        rt1 = view(AB, 3072, HALF, ROPE)
        probs1 = view(AB, 0, 2, 2, 384)
        pT1 = view(AB, 1536, 2, 3, 256)
        def catT_of(n):
            return view(AB, 0, KD, P) if n == 3 else view(W, 6144 + n % 2 * D, KD, P)

        junk = view(W, 9216, D)

        def tmp_of(n):
            at = 8192 if n < 3 else 5120
            return view(AB, 1024, D) if n == 3 else view(W, at, D)

        hp = view(W, 0, NT, KD, P)
        h2T = view(W, 3072, 2, KD, P)
        rows = view(W, 3072, 2, NT, 2 * SLOTS)
        silu = W[64:128, 4480:4736]
        hh = W[:, 4736:4992]
        hhT = view(W, 5120, 2, 2, SLOTS)
        ysb = view(W, 5376, 2, 512)
        def pair(t, k):
            return ring[:, 6 + t, k * D:(k + 1) * D]

        slotm = view(W, 6400, NT, NB)
        RB = 6400 + NT * NB
        xT = view(W, 6656, 2, KD, 2 * SLOTS)

        def cond_of(t):
            return 0 if t == 0 else 1

        MIX0 = [(t, i) for t in range(NT) for i in range(4)]
        SWEEPS = [(s, hb, t) for s in range(2) for hb in range(2) for t in ((0,), (1, 2))[s]]

        def batches(l, sweep=None):
            if l == 0:
                return [(n, t, i) for n, (t, i) in enumerate(MIX0)]
            at = len(MIX0) + 4 * sweep
            return [(at + i, SWEEPS[sweep][2], i) for i in range(4)]

        PREPS = []
        for s in range(2):
            for hb in range(2):
                PREPS += [[("kv", s, hb, t, j) for j, t in enumerate(((0,), (3, 1, 2))[s])]
                          + [("q", s, hb, ((0,), (1, 2))[s][0], 0)]]
                if s == 1:
                    PREPS += [[("q", s, hb, 2, 0)]]
        PREP_AT = [sum(map(len, PREPS[:i])) for i in range(len(PREPS))]

        def bc_source(n):
            l, v, c, hf = n // 24, n % 24 // 4, n % 4 // 2, n % 2
            chunk = 2 * v + hf
            return l, chunk // 4, 32 * (chunk % 4), c, hf

        def bc_target(n):
            v, c, hf = n % 24 // 4, n % 4 // 2, n % 2
            if v % 3 == 2:
                return G[:, c, hf * 512:(hf + 1) * 512]
            at = ((1 - v % 3) * 2 + c) * D + hf * 512
            return AB[:, at:at + 512]

        def bc_bank(n):
            if n % 24 in range(8, 12):
                return 6
            return 2 + n % 2 if n % 24 in range(12, 20) else n % 4

        block = ctx.enter_context(nc.Block())

        @block.sync
        def _(sp):
            def free(unit):
                last = unit - RING
                if last >= U_MOE[0] and last < U_WIN1:
                    e, n = divmod(last - U_MOE[0], 3)
                    sp.wait_ge(S["up_done" if n < 2 else "down_done"], e + 1)
                elif last >= 0:
                    sp.wait_ge(S["units_used"], used(last))

            def load(unit, dst_floats, src, dims=None):
                slot = unit % RING
                free(unit)
                dst = ring[:, slot, 0:dst_floats]
                if dims:
                    dst = dst.rearrange("p (k n) -> p k n", k=dims)
                sp.dma_start(dst, src).then_inc(ring_full[slot], 16)

            def load_ada(l, r):
                rows_by_chunk = A[f"l{l}_w_ada"].rearrange("(p k) n -> k p n", k=KD)
                for k in range(KD):
                    load(U_ADA[l][r] + k, SLOT, rows_by_chunk[k, :, r * SLOT:(r + 1) * SLOT])

            def load_wo(l):
                for k in range(4):
                    load(U_WO[l] + k, 2 * D,
                         A[f"l{l}_w_o"][2 * k * P:(2 * k + 2) * P, :].rearrange("(k p) n -> p k n", p=P), 2)

            def load_expert(l, e, u, n):
                slot = 3 * u + n
                w = A[f"l{l}_{('w1', 'w3', 'w2')[n]}"]
                if n < 2:
                    src = w[bass.ds(e, 1)].rearrange("e (p k) f -> p (e k f)", k=KD)
                    dst = ring[:, slot, :]
                else:
                    src = w[bass.ds(e, 1)].rearrange("e (k p) d -> p (e k) d", p=P)
                    dst = ring[:, slot, :].rearrange("p (k d) -> p k d", k=2)
                sp.dma_start(dst, src).then_inc(ring_full[slot], 16)

            def load_experts(l):
                for u in range(4):
                    for n in range(3):
                        free(U_MOE[l] + 3 * u + n)
                        load_expert(l, u, u, n)
                with sp.Fori(1, NE // 4) as i:
                    for u in range(4):
                        for n in range(3):
                            sp.wait_ge(S["up_done" if n < 2 else "down_done"], i * 4 + (l * NE + u - 3))
                            load_expert(l, i * 4 + u, u, n)

            def overflow(l):
                sp.wait_ge(S["route_ready"], l + 1)
                count = sp.value_load(ovi[0:1, l, 15:16], min_val=0, max_val=OVER)
                sp.wait_ge(S["up_done"], (l + 1) * NE - 2)
                sp.wait_ge(S["down_done"], (l + 1) * NE - 2)
                with sp.Fori(0, OVER) as b:
                    with sp.If(b < count):
                        sp.wait_ge(S[f"ov_free{l}"], b + 1)
                        e = sp.value_load(ovi[0:1, l, bass.ds(b, 1)], min_val=0, max_val=NE - 1)
                        for n, name in enumerate(("w1", "w3", "w2")):
                            w = A[f"l{l}_{name}"]
                            if n < 2:
                                src = w[bass.ds(e, 1)].rearrange("e (p k) f -> p (e k f)", k=KD)
                                dst = ring[:, 3 + n, :]
                            else:
                                src = w[bass.ds(e, 1)].rearrange("e (k p) d -> p (e k) d", p=P)
                                dst = ring[:, 3 + n, :].rearrange("p (k d) -> p k d", k=2)
                            sp.dma_start(dst, src).then_inc(S[f"ov_w{l}"], 16)
                        sp.sem_inc(S["ov_turns_sp"], 1)
                    sp.end_ifs()

            early_loads = ((cT[:, 0, :], A["c_ctx"].rearrange("(p k) -> p k", p=P)),
                           (cT[:, 1, :], A["c"].rearrange("a (p k) -> p (a k)", p=P)))
            for dst, src in early_loads:
                sp.dma_start(dst, src).then_inc(S["cond_in"], 16)
            w_in = A["l0_w_in"].rearrange("(u k p) n -> u p k n", k=2, p=P)
            load_ada(0, 0)
            for u in range(4):
                load(U_WIN_UV + u, 2 * UV, w_in[u, :, :, 0:UV], 2)
            load_ada(0, 1)
            for u in range(4):
                load(U_WIN_QK + u, 2 * QKV, w_in[u, :, :, UV:], 2)
            load_ada(0, 2)
            for r in range(3):
                load_ada(1, r)
            load_wo(0)
            load_experts(0)
            overflow(0)
            for n, (k0, k1) in enumerate(((0, 3), (3, 6), (6, 8))):
                load(U_WIN1 + n, (k1 - k0) * ODD_IN,
                     A["l1_w_in"][k0 * P:k1 * P, :].rearrange("(k p) n -> p k n", p=P), k1 - k0)
            sp.wait_ge(S["moe_done_gather"], 1)
            sp.wait_ge(S["x_updated"], 6)
            for k in range(3):
                load(U_UQ + k, C_HEADS * QK, A["l1_w_uq"][k * P:(k + 1) * P, :])
            for k in range(2):
                load(U_UKV + k, SLOT, A["l1_w_ukv"][k * P:(k + 1) * P, :])
            load_wo(1)
            load_experts(1)
            overflow(1)

        @block.tensor
        def _(pe):
            def arrived(unit):
                pe.wait_ge(ring_full[unit % RING], 16 * (unit // RING + 1))

            def ada_unit(l, n):
                r, k = divmod(n, KD)
                unit = U_ADA[l][r] + k
                arrived(unit)
                if n == 0 and l == 0:
                    pe.wait_ge(S["cond_ready"], 1)
                if k == 0 and 3 * l + r > 0:
                    pe.wait_ge(S["m_ready"], 3 * l + r)
                for j in range(4):
                    last = nc.tensor.matmul(ps[32 * j:32 * j + 32, 7, :], scT[:, k, :],
                                            ring[:, unit % RING, j * 512:(j + 1) * 512],
                                            start=k == 0, stop=k == KD - 1)
                last.then_inc(S["units_used"], 1)

            def broadcasts(first, count):
                for n in range(first, first + count):
                    l, r, row, c, hf = bc_source(n)
                    pe.wait_ge(S["m_ready"], 3 * l + r + 1)
                    bank = bc_bank(n)
                    before = [i for i in range(n) if bc_bank(i) == bank]
                    if before:
                        pe.wait_ge(S["bc_ready"], before[-1] + 1)
                    nc.tensor.matmul(ps[:, bank, :], con[row:row + 32, C_SEL + c * P:C_SEL + (c + 1) * P],
                                     m[row:row + 32, l, r, :], start=True, stop=True)\
                        .then_inc(S["bc_in_psum"], 1)

            def transpose_h(stage, src, t):
                pe.wait_ge(S["bc_ready"], 12 * stage + 8)
                pe.wait_ge(S["h_ready"], 3 * stage + t + 1)
                for k in range(KD):
                    chunk = src[:, t, k, :] if stage % 2 else src[:, t, k * P:(k + 1) * P]
                    last = nc.tensor.transpose(ps[:, 2 * t + k // 4, k % 4 * P:(k % 4 + 1) * P], chunk, ident)
                last.then_inc(S["hT_in_psum"], 1)

            def wait_hT(stage, tiles=NT):
                pe.wait_ge(S["hT_act"], 3 * stage + tiles)
                pe.wait_ge(S["hT_dve"], 3 * stage + tiles)

            def scores(l, b):
                gb, t, i = b
                if gb >= 2:
                    pe.wait_ge(S["probs_ready"], gb - 1)
                par = gb % 2
                nk = P if t == 0 else 384
                for hd in range(2):
                    out = ps[:, 2 * par + hd, 0:nk]
                    if l == 0:
                        half = slice(64 * hd, 64 * hd + 64)
                        key0 = 0 if t == 0 else 1
                        keys = kT0[half, key0:key0 + nk // P, :]
                        last = nc.tensor.matmul(out, qT0[half, t, i, :], keys, start=True, stop=True)
                    else:
                        head = 2 * i + hd
                        last = nc.tensor.matmul(out, qT1[0:QK, head, :], kT1[0:QK, head, 0:nk // P, :],
                                                start=True, stop=True)
                last.then_inc(S["scores_in_psum"], 1)

            def transpose_probs(l, b):
                gb, t, i = b
                par = gb % 2
                pe.wait_ge(S["probs_ready"], gb + 1)
                if gb >= 1:
                    pe.wait_ge(S["pT_act"], gb)
                    pe.wait_ge(S["pT_dve"], gb)
                probs = (probs0, probs1)[l]
                for kt in range(1 if t == 0 else 3):
                    for hd in range(2):
                        at = hd * 512 if t == 0 else (2 * kt + hd) * P
                        last = nc.tensor.transpose(ps[:, 4 + at // 512, at % 512:at % 512 + P],
                                                   probs[:, par, hd, kt * P:(kt + 1) * P], ident)
                last.then_inc(S["pT_in_psum"], 1)

            def weighted_values(l, b):
                gb, t, i = b
                par = gb % 2
                pe.wait_ge(S["pT_act"], gb + 1)
                pe.wait_ge(S["pT_dve"], gb + 1)
                if gb >= 1:
                    pe.wait_ge(S["att_ready"], gb)
                pT = (pT0, pT1)[l]
                tiles = 1 if t == 0 else 3
                for hd in range(2):
                    for kt in range(tiles):
                        if l == 0:
                            v = v0[:, kt + (0 if t == 0 else 1), hd * HD:(hd + 1) * HD]
                        else:
                            v = v1[:, kt, 2 * i + hd, :]
                        last = nc.tensor.matmul(ps[:, 6, hd * HD:(hd + 1) * HD],
                                                pT[:, par, kt, hd * P:(hd + 1) * P], v,
                                                start=kt == 0, stop=kt == tiles - 1)
                last.then_inc(S["att_in_psum"], 1)

            def attention(l, todo, between=None):
                scores(l, todo[0])
                for n, b in enumerate(todo):
                    if n + 1 < len(todo):
                        scores(l, todo[n + 1])
                    if between:
                        between(n)
                    transpose_probs(l, b)
                    if n:
                        weighted_values(l, todo[n - 1])
                weighted_values(l, todo[-1])

            def out_projection(l, n, t, src, release, rows=(0, 0)):
                base = 2 * (n % 2)
                catT = catT_of(n)
                pe.wait_ge(S["att_ready"], att_count(l, t))
                if n == 1:
                    pe.wait_ge(S["m_ready"], 6)
                for k in range(KD):
                    last = nc.tensor.transpose(ps[:, k // 4, k % 4 * P:(k % 4 + 1) * P],
                                               src[:, k * P:(k + 1) * P], ident)
                    if n == 4 and k == 0:
                        last.then_inc(S["units_used"], 5)
                last.then_inc(S["catT_in_psum"], 1)
                broadcasts(*rows)
                pe.wait_ge(S["catT_act"], n + 1)
                pe.wait_ge(S["catT_dve"], n + 1)
                for k in range(KD):
                    if t in (0, 1, 2) and k % 2 == 0:
                        arrived(U_WO[l] + k // 2)
                    for hf in range(2):
                        last = nc.tensor.matmul(ps[:, 4 + base + hf, :],
                                                catT[:, k, :],
                                                ring[:, (U_WO[l] + k // 2) % RING,
                                                     k % 2 * D + hf * 512:k % 2 * D + (hf + 1) * 512],
                                                start=k == 0, stop=k == KD - 1)
                    if release and k % 2:
                        last.then_inc(S["units_used"], 1)
                if not release:
                    last.then_inc(S["y_in_psum"], 1)

            def gather(n):
                for k in range(KD // 2):
                    for t in range(NT):
                        last = nc.tensor.matmul(ps[:, n % 2, k * P:(k + 1) * P],
                                                hp[:, t, n % 2 * (KD // 2) + k, :],
                                                rows[:, n // 2 % 2, t, :], start=t == 0, stop=t == NT - 1)
                return last

            def gather_one():
                for k in range(KD):
                    for t in range(NT):
                        last = nc.tensor.matmul(ps[:, 0, k * SLOTS:(k + 1) * SLOTS], hp[:, t, k, :],
                                                rows[:, 0, t, 0:SLOTS], start=t == 0, stop=t == NT - 1)
                return last

            def up(u, slot):
                par = u % 2
                mine = xT[:, u // 2, :, par * SLOTS:(par + 1) * SLOTS]
                for k in range(KD):
                    for n in range(2):
                        last = nc.tensor.matmul(ps[64 * n:64 * n + 64, 2 + par, 0:DE], mine[:, k, :],
                                                ring[:, slot + n, k * DE:(k + 1) * DE],
                                                start=k == 0, stop=k == KD - 1)
                return last

            def transpose_hh():
                for k in range(2):
                    last = nc.tensor.transpose(ps[:, 4, k * P:(k + 1) * P], hh[:, k * P:(k + 1) * P], ident)
                return last

            def down(par, slot):
                for k in range(2):
                    for n in range(2):
                        last = nc.tensor.matmul(ps[64 * n:64 * n + 64, 5 + par, :], hhT[:, par, k, :],
                                                ring[:, slot, k * D + n * 512:k * D + (n + 1) * 512],
                                                start=k == 0, stop=k == 1)
                return last

            def experts(l):
                base = l * NE
                turn = U_MOE[l] // RING

                def step(e, u, i, ahead=True):
                    par = u % 2
                    pe.wait_ge(S["xT_ready"], e + (base + 2 - par))
                    for n in range(2):
                        pe.wait_ge(ring_full[3 * u + n], i * 16 + 16 * (turn + 1))
                    up(u, 3 * u).then_inc(S["up_done"], 1)
                    if ahead:
                        pe.wait_ge(S["rows_ready"], e + (base + 4 - par))
                        gather((u + 2) % 4).then_inc(S["gathered"], 1)

                def down_step(e, u, i):
                    pe.wait_ge(S["hhT_ready"], e + (base + 1))
                    pe.wait_ge(ring_full[3 * u + 2], i * 16 + 16 * (turn + 1))
                    pe.wait_ge(S["y_evac"], e + (base + 1))
                    down(u % 2, 3 * u + 2).then_inc(S["down_done"], 1)

                def rest(e):
                    pe.wait_ge(S["hh_ready"], e + (base + 1))
                    transpose_hh().then_inc(S["hhT_in_psum"], 1)

                pe.wait_ge(S["rows_ready"], base + 2)
                for n in range(2):
                    gather(n).then_inc(S["gathered"], 1)
                step(0, 0, 0)
                rest(0)
                with pe.Fori(0, NE // 4 - 1) as i:
                    for u in range(4):
                        e = i * 4 + (u + 1)
                        v = (u + 1) % 4
                        step(e, v, i + (u + 1) // 4)
                        down_step(i * 4 + u, u, i)
                        rest(e)
                for e in range(NE - 3, NE):
                    step(e, e % 4, e // 4, e + 2 < NE)
                    down_step(e - 1, (e - 1) % 4, (e - 1) // 4)
                    rest(e)
                down_step(NE - 1, 3, NE // 4 - 1)

            def overflow(l):
                pe.wait_ge(S["route_ready"], l + 1)
                count = pe.value_load(ovi[0:1, l, 15:16], min_val=0, max_val=OVER)
                with pe.Fori(0, OVER) as b:
                    with pe.If(b < count):
                        pe.wait_ge(S[f"ov_rows{l}"], b + 1)
                        gather_one().then_inc(S[f"ov_gathered{l}"], 1)
                        pe.wait_ge(S[f"ov_xT{l}"], b + 1)
                        pe.wait_ge(S[f"ov_w{l}"], b * 48 + 48)
                        up(0, 3).then_inc(S[f"ov_h{l}"], 1)
                        pe.wait_ge(S[f"ov_hh{l}"], b + 1)
                        transpose_hh().then_inc(S[f"ov_hhT{l}"], 1)
                        pe.wait_ge(S[f"ov_hhTs{l}"], b + 1)
                        down(0, 5).then_inc(S[f"ov_y{l}"], 1)
                    pe.end_ifs()

            def router(l):
                def logits(t):
                    wait_hT(2 * l + 1, t + 1)
                    for k in range(KD):
                        last = nc.tensor.matmul(ps[:, 6, t * 36:(t + 1) * 36], h2T[:, t % 2, k, :],
                                                wr[:, l, k, :], start=k == 0, stop=k == KD - 1)
                    last.then_inc(S["logits_in_psum"], 1)

                transpose_h(2 * l + 1, hp, 0)
                transpose_h(2 * l + 1, hp, 1)
                logits(0)
                logits(1)
                transpose_h(2 * l + 1, hp, 2)
                logits(2)
                broadcasts(24 * l + 20, 12 if l == 0 else 4)
                pe.wait_ge(S["bc_ready"], 32 if l == 0 else 48)
                pe.wait_ge(S["picks_ready"], l + 1)
                picks = view(W, RB, NT, NE)
                tri = con[:, C_TRI:C_TRI + P]
                for t in range(NT):
                    for s in range(t + 1):
                        nc.tensor.matmul(ps[:, 7, t * NE:(t + 1) * NE], tri if s == t else ones[:, :],
                                         picks[:, s, :], start=s == 0, stop=s == t)
                for s in range(NT):
                    last = nc.tensor.matmul(ps[:, 7, NT * NE:(NT + 1) * NE], ones[:, :], picks[:, s, :],
                                            start=s == 0, stop=s == NT - 1)
                last.then_inc(S["rank_in_psum"], 1)
                pe.wait_ge(S["nover_ready"], l + 1)
                nc.tensor.matmul(ps[:, 6, 0:NE], view(W, RB + 300, P)[0:NE, :], con[0:NE, C_TRI:C_TRI + NE],
                                 start=True, stop=True).then_inc(S["ofs_in_psum"], 1)

            def att_count(l, t):
                if l == 0:
                    return 4 * (t + 1)
                last = max(n for n, w in enumerate(SWEEPS) if w[2] == t)
                return len(MIX0) + 4 * (last + 1)

            for n in range(KD):
                ada_unit(0, n)
            pe.wait_ge(S["early_in"], EARLY * 16)
            broadcasts(0, 8)
            pe.wait_ge(S["late_in"], LATE * 16)
            pe.wait_ge(S["tiles_cleared"], 2)
            for g in range(A_GROUPS):
                last = nc.tensor.transpose(ps[:, 6, g * P:(g + 1) * P], ws[:, g, :], ident)
            last.then_inc(S["ws_in_psum"], 1)
            pe.wait_ge(S["ws_ready"], 1)
            nc.tensor.transpose(ps[:, 6, 0:P], kc[:, :], ident).then_inc(S["kc_in_psum"], 1)
            for t in range(NT):
                transpose_h(0, h3, t)

            def project0(first, width, columns, signal):
                for k in range(KD):
                    unit = first + k // 2
                    arrived(unit)
                    for t in range(NT):
                        for n, (c0, c1) in enumerate(columns):
                            at = k % 2 * width
                            last = nc.tensor.matmul(ps[:, 2 * t + n, 0:c1 - c0], hT[:, t, k, :],
                                                    ring[:, unit % RING, at + c0:at + c1],
                                                    start=k == 0, stop=k == KD - 1)
                    if k % 2:
                        last.then_inc(S["units_used"], 1)

            wait_hT(0)
            project0(U_WIN_UV, UV, ((0, 512), (512, 1024)), None)
            for n in range(KD, 2 * KD):
                ada_unit(0, n)
            pe.wait_ge(S["gelu_done"], 1)
            project0(U_WIN_QK, QKV, ((0, 512), (512, QKV)), None)
            pe.wait_ge(S["kc_ready"], 1)
            broadcasts(8, 4)
            pe.wait_ge(S["bc_ready"], 12)
            for t in range(NT):
                pe.wait_ge(S["v_ready"], t + 1)
                if t:
                    pe.wait_ge(S["a_ready"], t)
                for g in range(A_GROUPS):
                    last = nc.tensor.matmul(ps[:, 6, g * P:(g + 1) * P], wsT[:, g, :],
                                            va[:, t, g * P:(g + 1) * P], start=True, stop=True)
                last.then_inc(S["mixed_in_psum"], 1)
                for n in range(2 * KD + 2 * t, 2 * KD + 2 * t + 2):
                    ada_unit(0, n)
            for t in range(NT):
                if t == 0:
                    ada_unit(0, 3 * KD - 2)
                    ada_unit(0, 3 * KD - 1)
                pe.wait_ge(S["qk_ready"], t + 1)
                pe.wait_ge(S["z_act_done"], t + 1)
                for i in range(5):
                    out = ps[:, 2 * t, i * P:(i + 1) * P] if i < 4 else ps[:, 2 * t + 1, 0:P]
                    last = nc.tensor.transpose(out, qk[:, i * P:(i + 1) * P], ident)
                last.then_inc(S["qkT_in_psum"], 1)
            pe.wait_ge(S["qkT_ready"], 3)
            pe.wait_ge(S["a_ready"], 3)
            attention(0, batches(0), lambda n: [ada_unit(1, 2 * n), ada_unit(1, 2 * n + 1)])
            for t in range(NT):
                out_projection(0, t, t, cat0[:, t, :], t == 2, ((12, 4), (16, 4), (0, 0))[t])
            router(0)
            experts(0)
            overflow(0)

            for t in range(NT):
                transpose_h(2, h3, t)
                wait_hT(2, t + 1)
                for k in range(KD):
                    u, c = divmod(k, 3)
                    arrived(U_WIN1 + u)
                    for n, (c0, c1) in enumerate(((0, Q_LORA), (Q_LORA, ODD_IN))):
                        last = nc.tensor.matmul(ps[:, 2 * t + n, 0:c1 - c0], hT[:, t, k, :],
                                                ring[:, (U_WIN1 + u) % RING, c * ODD_IN + c0:c * ODD_IN + c1],
                                                start=k == 0, stop=k == KD - 1)
                    if t == 2 and k in (2, 5, 7):
                        last.then_inc(S["units_used"], 1)
                if t < 2:
                    last.then_inc(S["z1_in_psum"], 1)
            pe.wait_ge(S["cache_in"], 32)
            for t in (3, 0, 1, 2):
                if t < 3:
                    pe.wait_ge(S["cqkv_ready"], t + 1)
                    for k in range(3):
                        nc.tensor.transpose(ps[:, 2 * t, k * P:(k + 1) * P], cqn[:, t, k * P:(k + 1) * P], ident)
                for k in range(2):
                    src = ckvc if t == 3 else ckvn[:, t, :]
                    last = nc.tensor.transpose(ps[:, 2 * t + (t < 3), k * P:(k + 1) * P],
                                               src[:, k * P:(k + 1) * P], ident)
                last.then_inc(S["cqkvT_in_psum"], 1)

            def expand(n, prep):
                kind, s, hb, t, j = prep
                base = 2 * (n % 2)
                if kind == "kv":
                    for k in range(2):
                        arrived(U_UKV + k)
                        for q in range(2):
                            at = hb * 1024 + q * 512
                            last = nc.tensor.matmul(ps[:, base + q, :], ckvT[:, t, k, :],
                                                    ring[:, (U_UKV + k) % RING, at:at + 512],
                                                    start=k == 0, stop=k == 1)
                else:
                    for k in range(3):
                        arrived(U_UQ + k)
                        for q in range(2):
                            at = hb * 768 + q * 384
                            last = nc.tensor.matmul(ps[:, base + q, 0:384], cqT[:, t, k, :],
                                                    ring[:, (U_UQ + k) % RING, at:at + 384],
                                                    start=k == 0, stop=k == 2)
                last.then_inc(S["prep_in_psum"], 1)

            def transpose_prep(n):
                pe.wait_ge(S["prep_ready"], n + 1)
                if n >= 2:
                    pe.wait_ge(S["prepT_act"], n - 1)
                    pe.wait_ge(S["prepT_dve"], n - 1)
                for h in range(HALF):
                    last = nc.tensor.transpose(ps[0:QK, 4 + 2 * (n % 2) + h // 4, h % 4 * P:(h % 4 + 1) * P],
                                               kw[:, h, :], ident)
                last.then_inc(S["prepT_in_psum"], 1)

            pe.wait_ge(S["cqkvT_ready"], 4)
            broadcasts(32, 4)
            pe.wait_ge(S["bc_ready"], 36)
            for sweep, preps in enumerate(PREPS):
                at = PREP_AT[sweep]
                expand(at, preps[0])
                for n, prep in enumerate(preps):
                    if n + 1 < len(preps):
                        expand(at + n + 1, preps[n + 1])
                    transpose_prep(at + n)
                pe.wait_ge(S["prepT_act"], at + len(preps))
                pe.wait_ge(S["prepT_dve"], at + len(preps))
                attention(1, batches(1, sweep))
                if sweep == 1:
                    out_projection(1, 3, 0, cat1[:, 0, :], False)
            for t in (1, 2):
                out_projection(1, 3 + t, t, cat1[:, t - 1, :], t == 2, (32 + 4 * t, 4))
            router(1)
            experts(1)
            overflow(1)

        @block.scalar
        def _(act):
            chain = [0]

            def link(ins):
                chain[0] += 1
                ins.then_inc(S["act_chain"], 1)
                act.wait_ge(S["act_chain"], chain[0])

            def spread(vec, n):
                return vec.rearrange("(a n) -> a n", a=1).to_broadcast([P, n])

            def early(dst, src):
                act.dma_start(dst, src).then_inc(S["early_in"], 16)

            def late(dst, src):
                act.dma_start(dst, src).then_inc(S["late_in"], 16)

            early(con[:, :], A["shape_constants"])
            act.wait_ge(S["tiles_cleared"], 1)
            for l in range(N_LAYERS):
                bias = A[f"l{l}_b_ada"].rearrange("(r j n) -> j r n", r=3, j=4)
                for j in range(4):
                    early(m[32 * j:32 * j + 2, l], bias[j:j + 1].to_broadcast([2, 3, 512]))
                for row, name, hf in ((0, "g_norm2", 0), (32, "g_norm2", 1), (64, "g_norm1", 0), (96, "g_norm1", 1)):
                    early(gn[row:row + 2, l], A[f"l{l}_{name}"][hf * 512:(hf + 1) * 512]
                          .rearrange("(a n) -> a n", a=1).to_broadcast([2, 512]))
            late(x[:, 0, :], A["x_prompt"].rearrange("a s d -> (a s) d"))
            late(x[:, 1:3, :], A["x_sample"].rearrange("a (t s) d -> s (a t) d", t=2))
            late(ws[:, :, :], A["l0_w_s"].rearrange("g t s -> t g s"))
            late(kc[:, :], A["cache_l0_k"].rearrange("a s h d -> (a s) (h d)"))
            late(v0[:, 1, :], A["cache_l0_v"].rearrange("a s h d -> (a s) (h d)"))
            late(gvn[:, :], spread(A["l0_g_vnorm"], A_WIDTH))
            for n in range(B_HEADS + 2):
                late(gqk[:, n * HD:(n + 1) * HD], spread(A["l0_g_q" if n < B_HEADS else "l0_g_k"], HD))
            with nc.allow_non_contiguous_dma(reason="512 words"):
                late(bsT[:, :], A["l0_b_s"].rearrange("g t -> t g"))
            late(sink[:, :], spread(A["l0_sink"], B_HEADS))
            late(gqa[:, :], spread(A["l1_g_qa"], Q_LORA))
            late(gkva[:, :], spread(A["l1_g_kva"], KV_LORA))
            late(gq1[:, :], spread(A["l1_g_q"], QK))
            late(gk1[:, :], spread(A["l1_g_k"], QK))
            for l in range(N_LAYERS):
                late(wr[:, l, :, 0:NG], A[f"l{l}_w_rg"].rearrange("(p k) n -> p k n", k=KD))
                late(wr[:, l, :, NG:], A[f"l{l}_w_re"].rearrange("(p k) n -> p k n", k=KD))
                late(br[:, l, 0:NG], spread(A[f"l{l}_b_rg"], NG))
                late(br[:, l, NG:], spread(A[f"l{l}_b_re"], NE))

            act.wait_ge(S["cond_in"], 32)
            act.wait_ge(S["tiles_cleared"], 2)
            nc.scalar.activation(scT[:, :, 0:2], cT[:, :, :].rearrange("p c k -> p k c"), ACT.Silu)\
                .then_inc(S["cond_ready"], 1)
            def rms(stage, tiles=range(NT)):
                for t in tiles:
                    if stage:
                        act.wait_ge(S["x_updated"], 3 * stage + t - 2)
                    squares = view(W, t * D, D) if stage % 2 else h3[:, t, :]
                    link(nc.scalar.activation(squares, x[:, t, :], ACT.Square, accum_out=ss[:, t:t + 1]))
                    nc.scalar.activation(ss[:, 4 + t:5 + t], ss[:, t:t + 1], ACT.Sqrt, bias=eps[:, :],
                                         scale=1.0 / D).then_inc(S["rms_ready"], 1)

            def broadcasts(first, count):
                for n in range(first, first + count):
                    if n in (20, 32, 44):
                        act.wait_ge(S["x_updated"], n // 12 * 3)
                    elif n == 24:
                        act.wait_ge(S["h_ready"], 6)
                    elif n in (12, 36):
                        act.wait_ge(S["att_ready"], len(MIX0) if n == 12 else len(MIX0) + 4 * len(SWEEPS))
                    act.wait_ge(S["bc_in_psum"], n + 1)
                    nc.scalar.copy(bc_target(n), ps[:, bc_bank(n), :]).then_inc(S["bc_ready"], 1)

            def evac_h(stage, dst, t):
                act.wait_ge(S["hT_in_psum"], 3 * stage + t + 1)
                if stage % 2 and t == 2:
                    act.wait_ge(S["logits_in_psum"], 3 * (stage // 2) + 1)
                nc.scalar.copy(dst[:, t % 2 if stage % 2 else t, 0:4, :],
                               ps[:, 2 * t, :].rearrange("p (k q) -> p k q", k=4)).then_inc(S["hT_act"], 1)

            def evac_qkT(t):
                act.wait_ge(S["qkT_in_psum"], t + 1)
                nc.scalar.copy(qT0[:, t, :, :], ps[:, 2 * t, :].rearrange("p (i q) -> p i q", i=4))
                nc.scalar.copy(kT0[:, 0 if t == 0 else t + 1, :], ps[:, 2 * t + 1, 0:P]).then_inc(S["qkT_ready"], 1)

            def exps(l, b):
                gb, t, i = b
                par = gb % 2
                probs = (probs0, probs1)[l]
                nk = P if t == 0 else 384
                act.wait_ge(S["max_ready"], gb + 1)
                if gb >= 2:
                    act.wait_ge(S["pT_in_psum"], gb - 1)
                if l == 0:
                    nc.scalar.activation(st[:, gb % 4, 8:10], st[:, gb % 4, 6:8], ACT.Exp)
                scale = HD ** -0.5 if l == 0 else QK ** -0.5
                for hd in range(2):
                    last = nc.scalar.activation(probs[:, par, hd, 0:nk], ps[:, 2 * par + hd, 0:nk], ACT.Exp,
                                                bias=st[:, gb % 4, 4 + hd:5 + hd], scale=scale,
                                                accum_out=st[:, gb % 4, 10 + hd:11 + hd])
                last.then_inc(S["probs_ready"], 1)

            def evac_pT(l, b):
                gb, t, i = b
                par = gb % 2
                pT = (pT0, pT1)[l]
                act.wait_ge(S["pT_in_psum"], gb + 1)
                if gb >= 2:
                    act.wait_ge(S["att_in_psum"], gb - 1)
                if t == 0:
                    nc.scalar.copy(pT[:, par, 0, 0:P], ps[:, 4, 0:P]).then_inc(S["pT_act"], 1)
                else:
                    nc.scalar.copy(pT[:, par, 0:2, :], ps[:, 4, :].rearrange("p (k n) -> p k n", k=2))\
                        .then_inc(S["pT_act"], 1)

            def attention(l, todo):
                exps(l, todo[0])
                for n, b in enumerate(todo):
                    if n + 1 < len(todo):
                        exps(l, todo[n + 1])
                    evac_pT(l, b)

            def evac_cat(n):
                act.wait_ge(S["catT_in_psum"], n + 1)
                if n >= 2:
                    act.wait_ge(S["x_updated"], x_after(n - 2))
                nc.scalar.copy(catT_of(n)[:, 0:4, :],
                               ps[:, 0, :].rearrange("p (k q) -> p k q", k=4)).then_inc(S["catT_act"], 1)

            def experts(l):
                base = l * NE

                def gate(e, u):
                    act.wait_ge(S["up_done"], e + (base + 1))
                    nc.scalar.activation(silu, ps[0:64, 2 + u % 2, 0:DE], ACT.Silu).then_inc(S["silu_ready"], 1)

                def evac_hh(e, u):
                    act.wait_ge(S["hhT_in_psum"], e + (base + 1))
                    nc.scalar.copy(hhT[:, u % 2, :, :],
                                   ps[:, 4, 0:2 * P].rearrange("p (k s) -> p k s", k=2)[:, :, SLOTS:])\
                        .then_inc(S["hhT_ready"], 1)

                def store(e, u, i):
                    par = u % 2
                    act.wait_ge(S["down_done"], e + (base + 1))
                    act.wait_ge(S[f"y_out{par}"], i * 64 + 32 * (base // 2 + u // 2 + 1))
                    nc.scalar.copy(ysb[:, par, :], ps[:, 5 + par, :]).then_inc(S["y_evac"], 1)
                    act.wait_ge(S["y_evac"], e + (base + 3))
                    for n in range(2):
                        act.dma_start(Y[bass.ds(e * SLOTS, SLOTS), n * 512:(n + 1) * 512],
                                      ysb[64 * n:64 * n + 64, par, :]).then_inc(S[f"y_out{par}"], 16)

                gate(0, 0)
                evac_hh(0, 0)
                with act.Fori(0, NE // 4 - 1) as i:
                    for u in range(4):
                        e = i * 4 + (u + 1)
                        gate(e, u + 1)
                        store(i * 4 + u, u, i)
                        evac_hh(e, u + 1)
                for e in range(NE - 3, NE):
                    gate(e, e)
                    store(e - 1, (e - 1) % 4, (e - 1) // 4)
                    evac_hh(e, e)
                store(NE - 1, 3, NE // 4 - 1)

            def overflow(l):
                act.wait_ge(S["route_ready"], l + 1)
                count = act.value_load(ovi[0:1, l, 15:16], min_val=0, max_val=OVER)
                act.wait_ge(S["y_out0"], 32 * ((l + 1) * NE // 2 + 1))
                act.wait_ge(S["y_out1"], 32 * ((l + 1) * NE // 2 + 1))
                with act.Fori(0, OVER) as b:
                    with act.If(b < count):
                        act.wait_ge(S[f"ov_h{l}"], b + 1)
                        nc.scalar.activation(silu, ps[0:64, 2, 0:DE], ACT.Silu).then_inc(S[f"ov_silu{l}"], 1)
                        act.wait_ge(S[f"ov_hhT{l}"], b + 1)
                        nc.scalar.copy(hhT[:, 0, :, :], ps[:, 4, 0:2 * P].rearrange("p (k s) -> p k s", k=2)[:, :, SLOTS:])\
                            .then_inc(S[f"ov_hhTs{l}"], 1)
                        act.wait_ge(S[f"ov_y{l}"], b + 1)
                        nc.scalar.copy(ysb[:, 0, :], ps[:, 5, :]).then_inc(S[f"ov_evac{l}"], 1)
                        act.wait_ge(S[f"ov_evac{l}"], b + 1)
                        for n in range(2):
                            act.dma_start(Y[bass.ds(b * SLOTS + NE * SLOTS, SLOTS), n * 512:(n + 1) * 512],
                                          ysb[64 * n:64 * n + 64, 0, :]).then_inc(S[f"ov_out{l}"], 16)
                        act.wait_ge(S[f"ov_out{l}"], b * 32 + 32)
                        act.sem_inc(S["ov_turns_act"], 1)
                    act.end_ifs()
                act.sem_inc(S["moe_done_gather"], 1)

            def router(l):
                act.wait_ge(S["gexp_in"], l + 1)
                nc.scalar.activation(view(W, RB + 450, 12), view(W, RB + 450, 12), ACT.Exp).then_inc(S["gexp_out"], 1)
                act.wait_ge(S["eexp_in"], l + 1)
                nc.scalar.activation(view(W, RB + 470, 3), view(W, RB + 470, 3), ACT.Exp).then_inc(S["eexp_out"], 1)

            broadcasts(0, 8)
            act.wait_ge(S["late_in"], LATE * 16)
            rms(0)
            act.wait_ge(S["ws_in_psum"], 1)
            nc.scalar.copy(wsT[:, :, :], ps[:, 6, :].rearrange("p (g t) -> p g t", g=A_GROUPS))\
                .then_inc(S["ws_ready"], 1)
            act.wait_ge(S["kc_in_psum"], 1)
            nc.scalar.copy(kT0[:, 1, :], ps[:, 6, 0:P]).then_inc(S["kc_ready"], 1)
            for t in range(NT):
                evac_h(0, hT, t)
            act.wait_ge(S["units_used"], used(U_WIN_UV + 3))
            for t in range(NT):
                nc.scalar.activation(va[:, t, :], ps[:, 2 * t + 1, :], ACT.Gelu_apprx_tanh)\
                    .then_inc(S["v_in"], 1)
            for t in range(NT):
                last = nc.scalar.activation(ua[:, t, :], ps[:, 2 * t, :], ACT.Gelu_apprx_tanh)
            last.then_inc(S["gelu_done"], 1)
            act.wait_ge(S["var_ready"], 1)
            nc.scalar.activation(ss[:, 36:39], ss[:, 32:35], ACT.Sqrt, bias=eps[:, :]).then_inc(S["var_roots"], 1)
            act.wait_ge(S["units_used"], used(U_WIN_QK + 3))
            for t in range(NT):
                if t:
                    act.wait_ge(S["qk_ready"], t)
                nc.scalar.activation(sq0[:, 0:512], ps[:, 2 * t, :], ACT.Square, scale=HD ** -0.5)
                nc.scalar.activation(sq0[:, 512:640], ps[:, 2 * t + 1, 0:P], ACT.Square, scale=HD ** -0.5)
                nc.scalar.copy(v0[:, 0 if t == 0 else t + 1, :], ps[:, 2 * t + 1, P:2 * P])\
                    .then_inc(S["z_act_done"], 1)
                if t == 0:
                    act.wait_ge(S["z_act_done"], 1)
                    act.dma_start(O[3].rearrange("a s h d -> (a s) (h d)"), v0[:, 0, :]).then_inc(S["v_out"], 16)
                act.wait_ge(S["sums_ready"], t + 1)
                nc.scalar.activation(ss[:, 20:30], ss[:, 8:18], ACT.Sqrt, bias=eps[:, :]).then_inc(S["roots_ready"], 1)
                if t == 0:
                    broadcasts(8, 4)
                if t:
                    evac_qkT(t - 1)
            evac_qkT(2)
            attention(0, batches(0))
            evac_cat(0)
            broadcasts(12, 4)
            evac_cat(1)
            broadcasts(16, 4)
            rms(1, (0,))
            evac_cat(2)
            rms(1, (1,))
            evac_h(1, h2T, 0)
            rms(1, (2,))
            evac_h(1, h2T, 1)
            evac_h(1, h2T, 2)
            broadcasts(20, 4)
            router(0)
            broadcasts(24, 8)
            experts(0)
            overflow(0)

            act.dma_start(ckvc[:, :], A["cache_l1_ckv"].rearrange("a s d -> (a s) d")).then_inc(S["cache_in"], 16)
            act.dma_start(kpe[:, 3, :], A["cache_l1_kpe"].rearrange("a s d -> (a s) d")).then_inc(S["cache_in"], 16)
            for t in range(NT):
                rms(2, (t,))
                evac_h(2, hT, t)
            for t in range(NT):
                if t < 2:
                    act.wait_ge(S["z1_in_psum"], t + 1)
                else:
                    act.wait_ge(S["units_used"], used(U_WIN1 + 2))
                link(nc.scalar.activation(junk[:, 0:Q_LORA], ps[:, 2 * t, 0:Q_LORA], ACT.Square,
                                          scale=Q_LORA ** -0.5, accum_out=ss[:, t:t + 1]))
                link(nc.scalar.activation(junk[:, 0:KV_LORA], ps[:, 2 * t + 1, 0:KV_LORA], ACT.Square,
                                          scale=KV_LORA ** -0.5, accum_out=ss[:, 3 + t:4 + t]))
                link(nc.scalar.activation(junk[:, 0:ROPE], ps[:, 2 * t + 1, KV_LORA:KV_LORA + ROPE], ACT.Square,
                                          scale=QK ** -0.5, accum_out=ss[:, 32 + t:33 + t]))
                link(nc.scalar.copy(kpe[:, t, :], ps[:, 2 * t + 1, KV_LORA:KV_LORA + ROPE]))
            act.wait_ge(S["cache_in"], 32)
            link(nc.scalar.activation(junk[:, 0:ROPE], kpe[:, 3, :], ACT.Square,
                                      scale=QK ** -0.5, accum_out=ss[:, 35:36]))
            act.dma_start(O[5].rearrange("a s d -> (a s) d"), kpe[:, 0, :]).then_inc(S["v_out"], 16)
            nc.scalar.activation(ss[:, 8:14], ss[:, 0:6], ACT.Sqrt, bias=eps[:, :]).then_inc(S["z1_roots"], 1)
            for n, t in enumerate((3, 0, 1, 2)):
                act.wait_ge(S["cqkvT_in_psum"], n + 1)
                if t < 3:
                    nc.scalar.copy(cqT[:, t, :, :], ps[:, 2 * t, 0:Q_LORA].rearrange("p (k q) -> p k q", k=3))
                nc.scalar.copy(ckvT[:, t, :, :],
                               ps[:, 2 * t + (t < 3), 0:KV_LORA].rearrange("p (k q) -> p k q", k=2))\
                    .then_inc(S["cqkvT_ready"], 1)

            broadcasts(32, 4)

            def square_prep(n, prep):
                kind, s, hb, t, j = prep
                base = 2 * (n % 2)
                act.wait_ge(S["prep_in_psum"], n + 1)
                if n:
                    act.wait_ge(S["prep_sums"], n)
                else:
                    act.wait_ge(S["l1_out"], 16)
                if n == PREP_AT[2]:
                    act.wait_ge(S["x_updated"], x_after(3))
                if kind == "kv":
                    kv = ps[:, base:base + 2, :].rearrange("p b (h c) -> p (b h) c", c=NOPE * 2)
                    nc.scalar.activation(sq1[:, :, 0:NOPE], kv[:, :, 0:NOPE], ACT.Square, scale=QK ** -0.5)\
                        .then_inc(S["prep_squares"], 1)
                    link(nc.scalar.copy(v1[:, j, :, :], kv[:, :, NOPE:]))
                else:
                    nc.scalar.activation(sq1[:, :, :].rearrange("p (b h) c -> p b (h c)", b=2),
                                         ps[:, base:base + 2, 0:384], ACT.Square, scale=QK ** -0.5)\
                        .then_inc(S["prep_squares"], 1)
                act.wait_ge(S["prep_sums"], n + 1)
                nc.scalar.activation(ss[:, 48:56], ss[:, 40:48], ACT.Sqrt, bias=eps[:, :])\
                    .then_inc(S["prep_roots"], 1)

            def evac_prep(n, prep):
                kind, s, hb, t, j = prep
                act.wait_ge(S["prepT_in_psum"], n + 1)
                src = ps[0:QK, 4 + 2 * (n % 2), :].rearrange("p (h q) -> p h q", h=4)
                dst = kT1[0:QK, 0:4, j, :] if kind == "kv" else qT1[0:QK, 0:4, :]
                nc.scalar.copy(dst, src).then_inc(S["prepT_act"], 1)

            for sweep, preps in enumerate(PREPS):
                at = PREP_AT[sweep]
                for n, prep in enumerate(preps):
                    square_prep(at + n, prep)
                    if n:
                        evac_prep(at + n - 1, preps[n - 1])
                evac_prep(at + len(preps) - 1, preps[-1])
                attention(1, batches(1, sweep))
                if sweep == 1:
                    evac_cat(3)
            evac_cat(4)
            broadcasts(36, 4)
            evac_cat(5)
            broadcasts(40, 4)
            rms(3, (0, 1))
            evac_h(3, h2T, 0)
            rms(3, (2,))
            evac_h(3, h2T, 1)
            evac_h(3, h2T, 2)
            broadcasts(44, 4)
            router(1)
            experts(1)
            overflow(1)
            act.wait_ge(S["x_updated"], 12)
            act.dma_start(O[0].rearrange("a s d -> (a s) d"), x[:, 0, :]).then_inc(S["out_done"], 16)
            act.dma_start(O[1].rearrange("a (t s) d -> s (a t) d", t=2), x[:, 1:3, :]).then_inc(S["out_done"], 16)
            act.wait_ge(S["out_done"], 2 * 16)
            act.wait_ge(S["k_out"], 16)
            act.wait_ge(S["l1_out"], 16)

        @block.vector
        def _(dve):
            V = nc.vector
            chain = [0]

            def link(ins):
                chain[0] += 1
                ins.then_inc(S["dve_chain"], 1)
                dve.wait_ge(S["dve_chain"], chain[0])

            def modulation(l, r):
                dve.wait_ge(S["units_used"], used(U_ADA[l][r] + KD - 1))
                row = m[:, l, r, :]
                if r == 1:
                    V.tensor_tensor(row, ps[:, 7, :], row, ALU.add).then_inc(S["m_ready"], 1)
                    return
                link(V.tensor_tensor(row, ps[:, 7, :], row, ALU.add))
                half = slice(64, 128) if r == 0 else slice(0, 64)
                V.scalar_tensor_tensor(out=m[half, l, r, :], in0=m[half, l, r, :], scalar=1.0,
                                       in1=gn[half, l, :], op0=ALU.add, op1=ALU.mult).then_inc(S["m_ready"], 1)

            def norm(stage, t):
                l, second = divmod(stage, 2)
                dve.wait_ge(S["bc_ready"], 24 * l + 12 * second + 8)
                dve.wait_ge(S["rms_ready"], 3 * stage + t + 1)
                link(V.reciprocal(ss[:, 8 + t:9 + t], ss[:, 4 + t:5 + t]))
                c = cond_of(t)
                a, b = AB[:, c * D:(c + 1) * D], AB[:, (2 + c) * D:(3 + c) * D]
                mid = tmp_of(4 * l) if second else h3[:, t, :]
                link(V.scalar_tensor_tensor(out=mid, in0=x[:, t, :], scalar=ss[:, 8 + t:9 + t], in1=a,
                                            op0=ALU.mult, op1=ALU.mult))
                if second:
                    V.tensor_tensor(hp[:, t, :, :].rearrange("p k q -> p q k"),
                                    mid.rearrange("p (q k) -> p q k", k=KD),
                                    b.rearrange("p (q k) -> p q k", k=KD), ALU.add).then_inc(S["h_ready"], 1)
                    dve.wait_ge(S["h_ready"], 3 * stage + t + 1)
                else:
                    V.tensor_tensor(mid, mid, b, ALU.add).then_inc(S["h_ready"], 1)

            def evac_h(stage, dst, t):
                dve.wait_ge(S["hT_in_psum"], 3 * stage + t + 1)
                if stage % 2 and t == 2:
                    dve.wait_ge(S["logits_in_psum"], 3 * (stage // 2) + 1)
                V.tensor_copy(dst[:, t % 2 if stage % 2 else t, 4:8, :],
                              ps[:, 2 * t + 1, :].rearrange("p (k q) -> p k q", k=4)).then_inc(S["hT_dve"], 1)

            def rope(xs, tmps, col, rot, heads):
                cos = over(con[:, col:col + rot], 1, [P, heads, rot])
                sin = con[:, col + rot:col + 2 * rot]
                for n in range(2):
                    link(V.tensor_tensor(tmps[:, :, n::2], xs[:, :, 1 - n::2],
                                         over(sin[:, n::2], 1, [P, heads, rot // 2]), ALU.mult))
                link(V.tensor_tensor(xs, xs, cos, ALU.mult))
                return V.tensor_tensor(xs, xs, tmps, ALU.add)

            def maxima(l, b):
                gb, t, i = b
                par = gb % 2
                nk = P if t == 0 else 384
                s = ps[:, 2 * par:2 * par + 2, 0:nk]
                dve.wait_ge(S["scores_in_psum"], gb + 1)
                if l == 0 and t:
                    at = 2 * P if t == 1 else P
                    part = ps[:, 2 * par:2 * par + 2, at:at + P]
                    mask = con[:, C_MASK + (t - 1) * P:C_MASK + t * P]
                    link(V.tensor_tensor(part, part, over(mask, 1, [P, 2, P]), ALU.add))
                link(V.tensor_reduce(st[:, gb % 4, 0:2], s, AX, ALU.max))
                if l == 0:
                    sk = sink[:, i:i + 5:4]
                    link(V.scalar_tensor_tensor(out=st[:, gb % 4, 2:4], in0=st[:, gb % 4, 0:2], scalar=HD ** -0.5,
                                                in1=sk, op0=ALU.mult, op1=ALU.max))
                    link(V.tensor_tensor(st[:, gb % 4, 6:8], sk, st[:, gb % 4, 2:4], ALU.subtract))
                    V.tensor_scalar(st[:, gb % 4, 4:6], st[:, gb % 4, 2:4], -1.0, None, ALU.mult)\
                        .then_inc(S["max_ready"], 1)
                else:
                    V.tensor_scalar(st[:, gb % 4, 4:6], st[:, gb % 4, 0:2], -QK ** -0.5, None, ALU.mult)\
                        .then_inc(S["max_ready"], 1)

            def evac_pT(l, b):
                gb, t, i = b
                par = gb % 2
                pT = (pT0, pT1)[l]
                dve.wait_ge(S["pT_in_psum"], gb + 1)
                if gb >= 2:
                    dve.wait_ge(S["att_in_psum"], gb - 1)
                if t == 0:
                    V.tensor_copy(pT[:, par, 0, P:2 * P], ps[:, 5, 0:P]).then_inc(S["pT_dve"], 1)
                else:
                    V.tensor_copy(pT[:, par, 2, :], ps[:, 5, 0:2 * P]).then_inc(S["pT_dve"], 1)

            def normalize(l, b):
                gb, t, i = b
                par = gb % 2
                dve.wait_ge(S["att_in_psum"], gb + 1)
                den = st[:, gb % 4, 10:12]
                if l == 0:
                    link(V.tensor_tensor(den, den, st[:, gb % 4, 8:10], ALU.add))
                link(V.reciprocal(st[:, gb % 4, 12:14], den))
                r = over(st[:, gb % 4, 12:14], 2, [P, 2, HD])
                if l == 0:
                    dst = cat0[:, t, 512:1024].rearrange("p (v i d) -> p v i d", v=2, i=4)[:, :, i, :]
                else:
                    sweep = (gb - len(MIX0)) // 4
                    at = SWEEPS[sweep][1] * 512 + i * P
                    dst = cat1[:, max(t - 1, 0), at:at + P].rearrange("p (v d) -> p v d", v=2)
                V.tensor_tensor(dst, ps[:, 6, 0:P].rearrange("p (v d) -> p v d", v=2), r, ALU.mult)\
                    .then_inc(S["att_ready"], 1)

            def attention(l, todo):
                maxima(l, todo[0])
                for n, b in enumerate(todo):
                    if n + 1 < len(todo):
                        maxima(l, todo[n + 1])
                    evac_pT(l, b)
                    if n:
                        normalize(l, todo[n - 1])
                normalize(l, todo[-1])

            def evac_cat(n):
                dve.wait_ge(S["catT_in_psum"], n + 1)
                if n >= 2:
                    dve.wait_ge(S["x_updated"], x_after(n - 2))
                if n == 5:
                    dve.wait_ge(S["v_out"], 32)
                V.tensor_copy(catT_of(n)[:, 4:8, :],
                              ps[:, 1, :].rearrange("p (k q) -> p k q", k=4)).then_inc(S["catT_dve"], 1)

            def residual(n, t, last_of_layer):
                if n == 0:
                    dve.wait_ge(S["fill_done"], 1)
                    dve.wait_ge(S["v_out"], 16)
                if last_of_layer is None:
                    dve.wait_ge(S["y_in_psum"], (1, 2, None, 3, 4)[n])
                else:
                    dve.wait_ge(S["units_used"], used(U_WO[last_of_layer] + 3))
                dve.wait_ge(S["bc_ready"], 24 * (n // 3) + 12)
                base = 4 + 2 * (n % 2)
                tmp = tmp_of(n)
                link(V.tensor_tensor(tmp, ps[:, base:base + 2, :].rearrange("p b n -> p (b n)"),
                                     G[:, cond_of(t), :], ALU.mult))
                V.tensor_tensor(x[:, t, :], x[:, t, :], tmp, ALU.add).then_inc(S["x_updated"], 1)
                dve.wait_ge(S["x_updated"], x_after(n))

            def first_max(src, pri, key, top, mask, n):
                link(V.tensor_reduce(top, src, AX, ALU.max))
                link(V.tensor_tensor(key, src, over(top, 2, [P, NT, n]), ALU.is_equal))
                link(V.tensor_tensor(key, key, over(pri, 1, [P, NT, n]), ALU.mult))
                link(V.tensor_reduce(ss[:, 60:63], key, AX, ALU.max))
                link(V.tensor_tensor(mask, key, over(ss[:, 60:63], 2, [P, NT, n]), ALU.is_equal))

            def router(l):
                at = [RB]

                def new(*shape):
                    at[0] += math.prod(shape)
                    return view(W, at[0] - math.prod(shape), *shape)

                picks = new(NT, NE)
                lg = new(NT, NG + NE)
                gmask = new(NT, NG)
                masks = [new(NT, EPG), new(NT, EPG)]
                at[0] = RB + 300
                spread = new(P)
                at[0] = RB + 450
                gexp = new(NT, NG)
                at[0] = RB + 470
                e21 = new(NT)
                key = new(NT, EPG)
                le = new(NT, EPG)
                top = [new(NT), new(NT), new(NT)]
                pg = new(NT)
                wk = new(NT, 2)
                wide = new(NT, NE)
                pick2 = [new(NT, NE), new(NT, NE)]
                rank = new(NT, NE)
                cnt = new(NE)
                nover = new(NE)
                ofs = new(NE)
                jumps = new(NT, NE)
                blk = new(NT, NE)
                mod = new(NT, NE)
                blks = new(2, NT)
                mods = new(2, NT)
                hit = new(NT, NB)
                obs = new(OVER, NE)
                obs2 = new(OVER, NE)
                obe = new(OVER)
                assert at[0] <= 10 * D
                lgg, lge = lg[:, :, 0:NG], lg[:, :, NG:]

                dve.wait_ge(S["logits_in_psum"], 3 * (l + 1))
                link(V.tensor_tensor(lg, ps[:, 6, 0:NT * 36].rearrange("p (t n) -> p t n", t=NT),
                                     over(br[:, l, :], 1, [P, NT, NG + NE]), ALU.add))
                first_max(lgg, con[:, C_PRI4:C_PRI4 + NG], key[:, :, 0:NG], top[0], gmask, NG)
                V.tensor_tensor(gexp, lgg, over(top[0], 2, [P, NT, NG]), ALU.subtract).then_inc(S["gexp_in"], 1)
                for t in range(NT):
                    last = V.tensor_tensor(wide[:, t, :].rearrange("p (g e) -> p g e", g=NG),
                                           lge[:, t, :].rearrange("p (g e) -> p g e", g=NG),
                                           over(gmask[:, t, :], 2, [P, NG, EPG]), ALU.mult)
                link(last)
                link(V.tensor_reduce(le, wide.rearrange("p t (g e) -> p t e g", g=NG), AX, ALU.add))
                first_max(le, con[:, C_PRI8:C_PRI8 + EPG], key, top[1], masks[0], EPG)
                link(V.scalar_tensor_tensor(out=le, in0=masks[0], scalar=NEG, in1=le, op0=ALU.mult, op1=ALU.add))
                first_max(le, con[:, C_PRI8:C_PRI8 + EPG], key, top[2], masks[1], EPG)
                V.tensor_tensor(e21, top[2], top[1], ALU.subtract).then_inc(S["eexp_in"], 1)
                for k in range(2):
                    for t in range(NT):
                        last = V.tensor_tensor(pick2[k][:, t, :].rearrange("p (g e) -> p g e", g=NG),
                                               over(gmask[:, t, :], 2, [P, NG, EPG]),
                                               over(masks[k][:, t, :], 1, [P, NG, EPG]), ALU.mult)
                link(last)
                V.tensor_tensor(picks, pick2[0], pick2[1], ALU.add).then_inc(S["picks_ready"], 1)
                dve.wait_ge(S["gexp_out"], l + 1)
                link(V.tensor_reduce(pg, gexp, AX, ALU.add))
                link(V.reciprocal(pg, pg))
                dve.wait_ge(S["eexp_out"], l + 1)
                link(V.tensor_scalar(wk[:, :, 0], e21, 1.0, None, ALU.add))
                link(V.reciprocal(wk[:, :, 0], wk[:, :, 0]))
                link(V.tensor_tensor(wk[:, :, 1], e21, wk[:, :, 0], ALU.mult))
                link(V.tensor_tensor(gates[:, :, :], wk, over(pg, 2, [P, NT, 2]), ALU.mult))
                dve.wait_ge(S["rank_in_psum"], l + 1)
                link(V.tensor_copy(rank, ps[:, 7, 0:NT * NE].rearrange("p (t n) -> p t n", t=NT)))
                link(V.tensor_copy(cnt, ps[:, 7, NT * NE:(NT + 1) * NE]))
                link(V.tensor_scalar(nover, cnt, float(SLOTS), None, ALU.is_gt))
                for n in range(2, MAX_BLOCKS):
                    link(V.scalar_tensor_tensor(out=nover, in0=cnt, scalar=float(SLOTS * n), in1=nover,
                                                op0=ALU.is_gt, op1=ALU.add))
                link(V.tensor_tensor(wide[:, 0, :], nover, con[:, C_ID:C_ID + NE], ALU.mult))
                link(V.tensor_reduce(ss[:, 63:64], wide[:, 0, :], AX, ALU.add))
                V.tensor_scalar(spread, ones[:, :], ss[:, 63:64], None, ALU.mult).then_inc(S["nover_ready"], 1)
                link(V.tensor_scalar(jumps, rank, float(SLOTS), None, ALU.is_ge))
                link(V.tensor_copy(blk, jumps))
                for n in range(2, MAX_BLOCKS):
                    link(V.scalar_tensor_tensor(out=jumps, in0=rank, scalar=float(SLOTS * n), in1=jumps,
                                                op0=ALU.is_ge, op1=ALU.add))
                link(V.scalar_tensor_tensor(out=mod, in0=jumps, scalar=-float(SLOTS), in1=rank,
                                            op0=ALU.mult, op1=ALU.add))
                dve.wait_ge(S["ofs_in_psum"], l + 1)
                link(V.tensor_copy(ofs, ps[:, 6, 0:NE]))
                link(V.tensor_tensor(wide[:, 0, :], ofs, con[:, C_31:C_31 + NE], ALU.add))
                link(V.tensor_tensor(blk, blk, over(wide[:, 0, :], 1, [P, NT, NE]), ALU.mult))
                link(V.tensor_tensor(blk, blk, jumps, ALU.add))
                link(V.tensor_tensor(blk, blk, over(iota[:, 0:NE], 1, [P, NT, NE]), ALU.add))
                for k in range(2):
                    for src, dst in ((blk, blks), (mod, mods)):
                        link(V.tensor_tensor(wide, pick2[k], src, ALU.mult))
                        link(V.tensor_reduce(dst[:, k, :], wide, AX, ALU.add))
                link(V.scalar_tensor_tensor(out=tabi[:, l, :].rearrange("p (k t) -> p k t", k=2), in0=blks,
                                            scalar=float(SLOTS), in1=mods, op0=ALU.mult, op1=ALU.add))
                link(V.tensor_scalar(mods, mods, 1.0, None, ALU.add))
                for k in range(2):
                    dst = slotm if k == 0 else hit
                    link(V.tensor_tensor(dst, over(iota[:, 0:NB], 1, [P, NT, NB]),
                                         over(blks[:, k, :], 2, [P, NT, NB]), ALU.is_equal))
                    link(V.tensor_tensor(dst, dst, over(mods[:, k, :], 2, [P, NT, NB]), ALU.mult))
                link(V.tensor_tensor(slotm, slotm, hit, ALU.add))
                link(V.tensor_scalar(slotm, slotm, -1.0, None, ALU.add))
                o1, n1 = ofs[0:1, :], nover[0:1, :]
                link(V.tensor_tensor(n1, n1, o1, ALU.add))
                bi = over(iota[0:1, 0:OVER], 2, [1, OVER, NE])
                link(V.tensor_tensor(obs[0:1], over(o1, 1, [1, OVER, NE]), bi, ALU.is_le))
                link(V.tensor_tensor(obs2[0:1], over(n1, 1, [1, OVER, NE]), bi, ALU.is_gt))
                link(V.tensor_tensor(obs[0:1], obs[0:1], obs2[0:1], ALU.mult))
                link(V.tensor_tensor(obs[0:1], obs[0:1], over(iota[0:1, 0:NE], 1, [1, OVER, NE]), ALU.mult))
                link(V.tensor_reduce(obe[0:1], obs[0:1], AX, ALU.add))
                link(V.tensor_copy(ovi[0:1, l, 0:OVER], obe[0:1]))
                V.tensor_copy(ovi[0:1, l, 15:16], n1[:, NE - 1:NE]).then_inc(S["route_ready"], 1)

            def one_hot(u, column, done):
                return V.tensor_tensor(rows[:, u // 2, :, u % 2 * SLOTS:(u % 2 + 1) * SLOTS], over(iota[:, 0:SLOTS], 1, [P, NT, SLOTS]),
                                       slotm[:, :, column].to_broadcast([P, NT, SLOTS]), ALU.is_equal)\
                    .then_inc(done, 1)

            def experts(l):
                base = l * NE

                def take_rows(n, count):
                    dve.wait_ge(S["gathered"], count)
                    half = slice(n % 2 * (KD // 2), (n % 2 + 1) * (KD // 2))
                    V.tensor_copy(xT[:, n // 2 % 2, half, :], ps[:, n % 2, :].rearrange("p (k s) -> p k s", s=P))\
                        .then_inc(S["xT_ready"], 1)

                def product(e, u):
                    dve.wait_ge(S["silu_ready"], e + (base + 1))
                    V.tensor_tensor(hh[64:128, :], silu, ps[64:128, 2 + u % 2, 0:DE], ALU.mult)\
                        .then_inc(S["hh_ready"], 1)

                link(V.memset(hh[0:64, :], 0.0))
                for e in range(4):
                    one_hot(e, slice(e, e + 1), S["rows_ready"])
                for n in range(2):
                    take_rows(n, base + n + 1)
                with dve.Fori(0, NE // 4 - 1) as i:
                    for u in range(4):
                        e = i * 4 + u
                        product(e, u)
                        take_rows((u + 2) % 4, e + (base + 3))
                        one_hot(u, bass.ds(e + 4, 1), S["rows_ready"])
                for e in range(NE - 4, NE):
                    product(e, e % 4)
                    if e + 2 < NE:
                        take_rows((e + 2) % 4, base + e + 3)

            def overflow(l):
                count = dve.value_load(ovi[0:1, l, 15:16], min_val=0, max_val=OVER)
                dve.wait_ge(S["gathered"], (l + 1) * NE)
                dve.wait_ge(S["xT_ready"], (l + 1) * NE)
                with dve.Fori(0, OVER) as b:
                    with dve.If(b < count):
                        one_hot(0, bass.ds(b + NE, 1), S[f"ov_rows{l}"])
                        dve.wait_ge(S[f"ov_gathered{l}"], b + 1)
                        V.tensor_copy(xT[:, 0, :, 0:SLOTS], ps[:, 0, :].rearrange("p (k s) -> p k s", k=KD))\
                            .then_inc(S[f"ov_xT{l}"], 1)
                        dve.wait_ge(S[f"ov_silu{l}"], b + 1)
                        V.tensor_tensor(hh[64:128, :], silu, ps[64:128, 2, 0:DE], ALU.mult).then_inc(S[f"ov_hh{l}"], 1)
                        dve.wait_ge(S[f"ov_y{l}"], b + 1)
                        dve.sem_inc(S[f"ov_free{l}"], 1)
                    dve.end_ifs()

            def combine(l, t):
                for k in range(2):
                    dve.wait_ge(S[f"pair_rows{2 * t + k}"], 16 * (l + 1))
                p0, p1 = pair(t, 0), pair(t, 1)
                link(V.tensor_scalar(p0, p0, gates[:, t, 0:1], None, ALU.mult))
                link(V.scalar_tensor_tensor(out=p0, in0=p1, scalar=gates[:, t, 1:2], in1=p0,
                                            op0=ALU.mult, op1=ALU.add))
                dve.wait_ge(S["bc_ready"], 24 * (l + 1))
                link(V.tensor_tensor(p0, p0, G[:, cond_of(t), :], ALU.mult))
                V.tensor_tensor(x[:, t, :], x[:, t, :], p0, ALU.add).then_inc(S["x_updated"], 1)
                dve.wait_ge(S["x_updated"], 6 * l + 4 + t)

            V.memset(m[:, :, :, :], 0.0)
            V.memset(gn[:, :, :], 0.0).then_inc(S["tiles_cleared"], 1)
            V.memset(scT[:, :, :], 0.0)
            V.memset(eps[:, :], EPS)
            V.memset(ones[:, :], 1.0).then_inc(S["tiles_cleared"], 1)
            def mixed():
                for t in range(NT):
                    dve.wait_ge(S["mixed_in_psum"], t + 1)
                    for g in range(A_GROUPS):
                        part = slice(g * P, (g + 1) * P)
                        last = V.scalar_tensor_tensor(out=cat0[:, t, part], in0=ps[:, 6, part],
                                                      scalar=bsT[:, g:g + 1], in1=ua[:, t, part],
                                                      op0=ALU.add, op1=ALU.mult)
                    last.then_inc(S["a_ready"], 1)

            dve.wait_ge(S["early_in"], EARLY * 16)
            modulation(0, 0)
            dve.wait_ge(S["late_in"], LATE * 16)
            for t in range(NT):
                norm(0, t)
            for t in range(NT):
                evac_h(0, hT, t)
            for t in range(NT):
                dve.wait_ge(S["v_in"], t + 1)
                link(V.bn_stats(ss[:, 40:46], va[:, t, :]))
                link(V.bn_aggr(ss[:, 46 + 2 * t:48 + 2 * t], ss[:, 40:46]))
            V.tensor_copy(ss[:, 32:35], ss[:, 47:53:2]).then_inc(S["var_ready"], 1)
            dve.wait_ge(S["var_roots"], 1)
            link(V.reciprocal(ss[:, 60:63], ss[:, 36:39]))
            for t in range(NT):
                v = va[:, t, :]
                link(V.tensor_scalar(v, v, ss[:, 46 + 2 * t:47 + 2 * t], ss[:, 60 + t:61 + t],
                                     ALU.subtract, ALU.mult))
                V.tensor_tensor(v, v, gvn[:, :], ALU.mult).then_inc(S["v_ready"], 1)
            modulation(0, 1)
            for t in range(NT):
                dve.wait_ge(S["z_act_done"], t + 1)
                V.tensor_reduce(ss[:, 8:18], sq0.rearrange("p (h d) -> p h d", h=B_HEADS + 2), AX, ALU.add)\
                    .then_inc(S["sums_ready"], 1)
                dve.wait_ge(S["roots_ready"], t + 1)
                link(V.reciprocal(ss[:, 44:54], ss[:, 20:30]))
                if t:
                    dve.wait_ge(S["qkT_in_psum"], t)
                if t == 1:
                    dve.wait_ge(S["k_out"], 16)
                for kv in range(2):
                    V.tensor_tensor(qk[:, 0:512].rearrange("p (i v d) -> p i v d", i=4, v=2)[:, :, kv, :],
                                    ps[:, 2 * t, kv * 256:(kv + 1) * 256].rearrange("p (i d) -> p i d", i=4),
                                    over(ss[:, 44 + 4 * kv:48 + 4 * kv], 2, [P, 4, HD]), ALU.mult)
                link(V.tensor_tensor(qk[:, 512:640].rearrange("p (v d) -> p v d", v=2),
                                     ps[:, 2 * t + 1, 0:P].rearrange("p (v d) -> p v d", v=2),
                                     over(ss[:, 52:54], 2, [P, 2, HD]), ALU.mult))
                heads = qk.rearrange("p (h d) -> p h d", d=HD)
                if t == 0:
                    V.tensor_tensor(qk, qk, gqk[:, :], ALU.mult).then_inc(S["qk_ready"], 1)
                else:
                    link(V.tensor_tensor(qk, qk, gqk[:, :], ALU.mult))
                    rope(heads, rt0.rearrange("p (h d) -> p h d", d=HD), C_R0 + (t - 1) * 2 * HD, HD,
                         B_HEADS + 2).then_inc(S["qk_ready"], 1)
                if t == 0:
                    mixed()
            modulation(0, 2)
            todo = batches(0)
            maxima(0, todo[0])
            for n, b in enumerate(todo):
                if n + 1 < len(todo):
                    maxima(0, todo[n + 1])
                evac_pT(0, b)
                if n:
                    normalize(0, todo[n - 1])
                if n % 4 == 3:
                    modulation(1, n // 4)
            normalize(0, todo[-1])
            evac_cat(0)
            residual(0, 0, None)
            evac_cat(1)
            norm(1, 0)
            residual(1, 1, None)
            evac_cat(2)
            norm(1, 1)
            residual(2, 2, 0)
            norm(1, 2)
            for t in range(NT):
                evac_h(1, h2T, t)
            router(0)
            dve.wait_ge(S["route_ready"], 1)
            experts(0)
            overflow(0)
            combine(0, 0)

            for t in range(NT):
                norm(2, t)
                evac_h(2, hT, t)
                if t + 1 < NT:
                    combine(0, t + 1)
            dve.wait_ge(S["z1_roots"], 1)
            link(V.reciprocal(ss[:, 16:22], ss[:, 8:14]))
            for t in range(NT):
                V.scalar_tensor_tensor(out=cqn[:, t, :], in0=ps[:, 2 * t, 0:Q_LORA], scalar=ss[:, 16 + t:17 + t],
                                       in1=gqa[:, :], op0=ALU.mult, op1=ALU.mult)
                V.scalar_tensor_tensor(out=ckvn[:, t, :], in0=ps[:, 2 * t + 1, 0:KV_LORA],
                                       scalar=ss[:, 19 + t:20 + t], in1=gkva[:, :], op0=ALU.mult,
                                       op1=ALU.mult).then_inc(S["cqkv_ready"], 1)

            def prep(n, p):
                kind, s, hb, t, j = p
                base = 2 * (n % 2)
                width = NOPE if kind == "kv" else QK
                dve.wait_ge(S["prep_squares"], n + 1)
                red = V.tensor_reduce(ss[:, 40:48], sq1[:, :, 0:width], AX, ALU.add)
                if kind == "kv":
                    link(red)
                    V.tensor_scalar(ss[:, 40:48], ss[:, 40:48], ss[:, 32 + t:33 + t], None, ALU.add)\
                        .then_inc(S["prep_sums"], 1)
                else:
                    red.then_inc(S["prep_sums"], 1)
                dve.wait_ge(S["prep_roots"], n + 1)
                if n:
                    dve.wait_ge(S["prepT_in_psum"], n)
                else:
                    dve.wait_ge(S["cqkvT_in_psum"], 4)
                    dve.wait_ge(S["l1_out"], 16)
                link(V.reciprocal(ss[:, 56:64], ss[:, 48:56]))
                rn = ss[:, 56:64]
                if kind == "kv":
                    kv = ps[:, base:base + 2, :].rearrange("p b (h c) -> p (b h) c", c=2 * NOPE)
                    V.tensor_tensor(kw[:, :, 0:NOPE], kv[:, :, 0:NOPE], over(rn, 2, [P, HALF, NOPE]), ALU.mult)
                    link(V.tensor_tensor(kw[:, :, NOPE:], over(kpe[:, t, :], 1, [P, HALF, ROPE]),
                                         over(rn, 2, [P, HALF, ROPE]), ALU.mult))
                else:
                    for q in range(2):
                        last = V.tensor_tensor(kw[:, 4 * q:4 * q + 4, :],
                                               ps[:, base + q, 0:384].rearrange("p (h c) -> p h c", c=QK),
                                               over(rn[:, 4 * q:4 * q + 4], 2, [P, 4, QK]), ALU.mult)
                    link(last)
                gain = over((gk1 if kind == "kv" else gq1)[:, :], 1, [P, HALF, QK])
                if t in (0, 3):
                    V.tensor_tensor(kw, kw, gain, ALU.mult).then_inc(S["prep_ready"], 1)
                else:
                    link(V.tensor_tensor(kw, kw, gain, ALU.mult))
                    rope(kw[:, :, NOPE:], rt1, C_R1 + (t - 1) * 2 * ROPE, ROPE, HALF).then_inc(S["prep_ready"], 1)

            def evac_prep(n, p):
                kind, s, hb, t, j = p
                dve.wait_ge(S["prepT_in_psum"], n + 1)
                src = ps[0:QK, 5 + 2 * (n % 2), :].rearrange("p (h q) -> p h q", h=4)
                dst = kT1[0:QK, 4:8, j, :] if kind == "kv" else qT1[0:QK, 4:8, :]
                V.tensor_copy(dst, src).then_inc(S["prepT_dve"], 1)

            for sweep, preps in enumerate(PREPS):
                at = PREP_AT[sweep]
                for n, p in enumerate(preps):
                    prep(at + n, p)
                    if n:
                        evac_prep(at + n - 1, preps[n - 1])
                evac_prep(at + len(preps) - 1, preps[-1])
                attention(1, batches(1, sweep))
                if sweep == 1:
                    evac_cat(3)
                    residual(3, 0, None)
            evac_cat(4)
            residual(4, 1, None)
            evac_cat(5)
            norm(3, 0)
            norm(3, 1)
            residual(5, 2, 1)
            norm(3, 2)
            for t in range(NT):
                evac_h(3, h2T, t)
            router(1)
            dve.wait_ge(S["route_ready"], 2)
            experts(1)
            overflow(1)
            for t in range(NT):
                combine(1, t)

        @block.gpsimd
        def _(pool):
            pool.sem_inc(S["y_evac"], 2)
            for par in range(2):
                pool.sem_inc(S[f"y_out{par}"], 32)
            for l in range(N_LAYERS):
                pool.sem_inc(S[f"ov_free{l}"], 1)
            pool.wait_ge(S["gelu_done"], 1)
            for n in range(0, OVER * SLOTS, P):
                count = min(P, OVER * SLOTS - n)
                pool.dma_start(Y[NE * SLOTS + n:NE * SLOTS + n + count, :], x[0:count, 0, :])\
                    .then_inc(S["filled"], 16)
            pool.wait_ge(S["filled"], 16 * (-(-OVER * SLOTS // P)))
            pool.sem_inc(S["fill_done"], 1)
            for l in range(N_LAYERS):
                if l == 0:
                    pool.wait_ge(S["qk_ready"], 1)
                    pool.dma_start(O[2].rearrange("a s h d -> (a s) (h d)"), qk[:, 512:640]).then_inc(S["k_out"], 16)
                else:
                    pool.wait_ge(S["cqkv_ready"], 1)
                    pool.dma_start(O[4].rearrange("a s d -> (a s) d"), ckvn[:, 0, :]).then_inc(S["l1_out"], 16)
                pool.wait_ge(S["route_ready"], l + 1)
                pool.wait_ge(S["moe_done_gather"], l + 1)
                pool.wait_ge(S["gathered"], (l + 1) * NE)
                for t in range(NT):
                    for k in range(2):
                        dst = pair(t, k)
                        idx = bass.IndirectOffsetOnAxis(tabi[:, l, 3 * k + t:3 * k + t + 1], 0)
                        done = S[f"pair_rows{2 * t + k}"]
                        pool.indirect_dma_start(dst, None, Y[:, :], idx).then_inc(done, 16)


def x_after(n):
    return n + 1 if n < 3 else n + 4


EARLY = 1 + N_LAYERS * 8
LATE = 6 + (B_HEADS + 2) + 6 + 4 * N_LAYERS


_CONSTS = "shape_constants"
_OUTS = [(1, P, D), (1, 2 * P, D), (1, P, 2, HD), (1, P, 2, HD), (1, P, KV_LORA), (1, P, ROPE)]


def kernel(**inputs):
    import concourse.bacc as bacc
    from concourse.bass_utils import run_bass_kernel_spmd

    nc = bacc.Bacc("TRN2", target_bir_lowering=False, num_devices=1)
    arrays = {"in_" + k: np.ascontiguousarray(v) for k, v in inputs.items()}
    arrays["in_" + _CONSTS] = shape_constants()
    A = {k[3:]: nc.dram_tensor(k, v.shape, mybir.dt.from_np(v.dtype), kind="ExternalInput").ap()
         for k, v in arrays.items()}
    O = [nc.dram_tensor(f"out_{i}", s, mybir.dt.float32, kind="ExternalOutput").ap() for i, s in enumerate(_OUTS)]
    Y = nc.dram_tensor("expert_rows", ((NE + OVER) * SLOTS, D), mybir.dt.float32).ap()
    trunk(nc, A, O, Y)
    r = run_bass_kernel_spmd(nc, [arrays], core_ids=[0])
    return tuple(r.results[0][f"out_{i}"] for i in range(len(_OUTS)))
```
